# Optimizing a Trainium2 kernel written in Bass

```python
import math
import jax, jax.numpy as jnp
from jax import lax
import numpy as np

D_MODEL = 1024
BATCH = 1
SEQ = 512
DEPTH = 1

CHUNK = 64
EPS = 1e-6
ATTN_HEADS = 16
ATTN_KV_HEADS = 4
HEAD_DIM = 64
WINDOW = 128
WINDOW_CHUNKS = WINDOW // CHUNK
ROPE_THETA = 10000.0
Q_W = ATTN_HEADS * HEAD_DIM
KV_W = ATTN_KV_HEADS * HEAD_DIM
SSD_INNER = 2 * D_MODEL
SSD_HEAD_DIM = 64
SSD_HEADS = SSD_INNER // SSD_HEAD_DIM
SSD_GROUPS = 4
SSD_HPG = SSD_HEADS // SSD_GROUPS
SSD_STATE = 128
SSD_CONV = 4
BC_W = SSD_GROUPS * SSD_STATE
SSD_CONV_DIM = SSD_INNER + 2 * BC_W
D_FF = 2816
FFN_CONV = 3
IN_WIDTHS = (Q_W, KV_W, KV_W, SSD_INNER, SSD_CONV_DIM, SSD_HEADS, D_MODEL, D_MODEL)
D_IN = sum(IN_WIDTHS)

kernel_name = "hybrid_swa_sink_ssd_convffn_block"

def _split(a, widths):
    outs, start = [], 0
    for w in widths:
        outs.append(a[..., start:start + w])
        start += w
    return outs

def rmsnorm(x, w):
    xf = x.astype(jnp.float32)
    y = xf * lax.rsqrt(jnp.mean(xf * xf, axis=-1, keepdims=True) + EPS)
    return (y * w.astype(jnp.float32)).astype(x.dtype)

def causal_dwconv(x, w, b):
    k_w = w.shape[0]
    s = x.shape[1]
    xp = jnp.pad(x, ((0, 0), (k_w - 1, 0), (0, 0)))
    out = b
    for k in range(k_w):
        out = out + xp[:, k:k + s] * w[k]
    return out

def rope(x, positions):
    half = HEAD_DIM // 2
    inv = 1.0 / (ROPE_THETA ** (jnp.arange(half, dtype=jnp.float32) * (2.0 / HEAD_DIM)))
    ang = positions.astype(jnp.float32)[..., None] * inv
    cos = jnp.cos(ang)[:, :, None, :]
    sin = jnp.sin(ang)[:, :, None, :]
    xf = x.astype(jnp.float32)
    x1, x2 = xf[..., :half], xf[..., half:]
    return jnp.concatenate([x1 * cos - x2 * sin, x2 * cos + x1 * sin], axis=-1).astype(x.dtype)

def banded_sink_attention(q, k, v, sinks):
    b, s = q.shape[:2]
    n_c = s // CHUNK
    rep = ATTN_HEADS // ATTN_KV_HEADS
    qc = q.reshape(b, n_c, CHUNK, ATTN_KV_HEADS, rep, HEAD_DIM)
    kc = k.reshape(b, n_c, CHUNK, ATTN_KV_HEADS, HEAD_DIM)
    vc = v.reshape(b, n_c, CHUNK, ATTN_KV_HEADS, HEAD_DIM)
    shifts = list(range(WINDOW_CHUNKS - 1, -1, -1))

    def band(t):
        return jnp.concatenate(
            [jnp.pad(t, ((0, 0), (sh, 0), (0, 0), (0, 0), (0, 0)))[:, :n_c] for sh in shifts], axis=2)

    kb, vb = band(kc), band(vc)
    key_shift = jnp.repeat(jnp.arange(WINDOW_CHUNKS - 1, -1, -1), CHUNK)
    valid = jnp.arange(n_c)[:, None] >= key_shift[None, :]
    scores = jnp.einsum('bcqgrd,bckgd->bcgrqk', qc, kb,
                        preferred_element_type=jnp.float32) * (1.0 / math.sqrt(HEAD_DIM))
    scores = jnp.where(valid[None, :, None, None, None, :], scores, -jnp.inf)
    sink = jnp.broadcast_to(sinks.astype(jnp.float32).reshape(1, 1, ATTN_KV_HEADS, rep, 1, 1),
                            scores.shape[:-1] + (1,))
    probs = jax.nn.softmax(jnp.concatenate([scores, sink], axis=-1), axis=-1)[..., :-1]
    out = jnp.einsum('bcgrqk,bckgd->bcqgrd', probs.astype(v.dtype), vb)
    return out.reshape(b, s, ATTN_HEADS * HEAD_DIM)

def ssd_mixer(z, xbc, dt_raw, conv_w, conv_b, dt_bias, a_log, d_skip, norm_w):
    b, s = z.shape[:2]
    n_c = s // CHUNK
    f32 = jnp.float32
    xbc = jax.nn.silu(causal_dwconv(xbc, conv_w, conv_b))
    xs, bm, cm = _split(xbc, (SSD_INNER, BC_W, BC_W))
    x = xs.astype(f32).reshape(b, n_c, CHUNK, SSD_GROUPS, SSD_HPG, SSD_HEAD_DIM)
    bm = bm.astype(f32).reshape(b, n_c, CHUNK, SSD_GROUPS, SSD_STATE)
    cm = cm.astype(f32).reshape(b, n_c, CHUNK, SSD_GROUPS, SSD_STATE)
    dt = jax.nn.softplus(dt_raw.astype(f32) + dt_bias.astype(f32))
    dt = dt.reshape(b, n_c, CHUNK, SSD_GROUPS, SSD_HPG)
    a = -jnp.exp(a_log.astype(f32)).reshape(SSD_GROUPS, SSD_HPG)
    a_dt = jnp.transpose(dt * a, (0, 3, 4, 1, 2))
    a_cs = jnp.cumsum(a_dt, axis=-1)
    xdt = x * dt[..., None]
    tri = jnp.tril(jnp.ones((CHUNK, CHUNK), dtype=bool))
    seg = a_cs[..., :, None] - a_cs[..., None, :]
    lmat = jnp.exp(jnp.where(tri, seg, -jnp.inf))
    cb = jnp.einsum('bclgn,bcsgn->bgcls', cm, bm)
    y_diag = jnp.einsum('bgjcls,bcsgjp->bclgjp', cb[:, :, None] * lmat, xdt)
    decay_states = jnp.transpose(jnp.exp(a_cs[..., -1:] - a_cs), (0, 3, 4, 1, 2))
    states = jnp.einsum('bcsgn,bcsgjp->bcgjpn', bm, xdt * decay_states[..., None])
    chunk_decay = jnp.exp(a_cs[..., -1])

    def step(carry, inp):
        st, dec = inp
        return carry * dec[..., None, None] + st, carry

    init = jnp.zeros((b, SSD_GROUPS, SSD_HPG, SSD_HEAD_DIM, SSD_STATE), f32)
    _, prev = lax.scan(step, init, (jnp.moveaxis(states, 1, 0), jnp.moveaxis(chunk_decay, 3, 0)))
    y_off = jnp.einsum('bclgn,cbgjpn->bclgjp', cm, prev)
    y_off = y_off * jnp.transpose(jnp.exp(a_cs), (0, 3, 4, 1, 2))[..., None]
    y = y_diag + y_off + x * d_skip.astype(f32).reshape(SSD_GROUPS, SSD_HPG)[:, :, None]
    y = y.reshape(b, s, SSD_INNER) * jax.nn.silu(z.astype(f32))
    yg = y.reshape(b, s, SSD_GROUPS, SSD_INNER // SSD_GROUPS)
    yg = yg * lax.rsqrt(jnp.mean(yg * yg, axis=-1, keepdims=True) + EPS)
    return (yg.reshape(b, s, SSD_INNER) * norm_w.astype(f32)).astype(z.dtype)

def setup_inputs(seed: int = 0) -> dict:
    key = jax.random.key(seed)
    ks = jax.random.split(key, 24)
    nrm = lambda k, shape, scale: jax.random.normal(k, shape, jnp.float32) * scale
    gain = lambda k, n: 1.0 + nrm(k, (DEPTH, n), 0.05)
    dt0 = jnp.exp(jax.random.uniform(ks[6], (DEPTH, SSD_HEADS), jnp.float32,
                                     math.log(1e-3), math.log(1e-1)))
    offsets = jax.random.randint(ks[1], (BATCH, 1), 0, 4096, dtype=jnp.int32)
    return {
        "x": nrm(ks[0], (BATCH, SEQ, D_MODEL), 1.0),
        "positions": offsets + jnp.arange(SEQ, dtype=jnp.int32)[None, :],
        "mix_pre_norm": gain(ks[2], D_MODEL),
        "w_in": nrm(ks[3], (DEPTH, D_MODEL, D_IN), D_MODEL ** -0.5),
        "attn_sinks": nrm(ks[4], (DEPTH, ATTN_HEADS), 0.5),
        "ssd_conv_w": nrm(ks[5], (DEPTH, SSD_CONV, SSD_CONV_DIM), SSD_CONV ** -0.5),
        "ssd_conv_b": nrm(ks[7], (DEPTH, SSD_CONV_DIM), 0.02),
        "ssd_dt_bias": dt0 + jnp.log(-jnp.expm1(-dt0)),
        "ssd_a_log": jnp.log(jax.random.uniform(ks[8], (DEPTH, SSD_HEADS), jnp.float32, 1.0, 16.0)),
        "ssd_d": 1.0 + nrm(ks[9], (DEPTH, SSD_HEADS), 0.05),
        "ssd_norm": gain(ks[10], SSD_INNER),
        "w_attn_out": nrm(ks[11], (DEPTH, Q_W, D_MODEL), Q_W ** -0.5),
        "w_ssd_out": nrm(ks[12], (DEPTH, SSD_INNER, D_MODEL), SSD_INNER ** -0.5),
        "w_out": nrm(ks[13], (DEPTH, D_MODEL, D_MODEL), D_MODEL ** -0.5),
        "mix_post_norm": gain(ks[14], D_MODEL),
        "ffn_pre_norm": gain(ks[15], D_MODEL),
        "w_up": nrm(ks[16], (DEPTH, D_MODEL, 2 * D_FF), D_MODEL ** -0.5),
        "ffn_conv_w": nrm(ks[17], (DEPTH, FFN_CONV, 2 * D_FF), FFN_CONV ** -0.5),
        "ffn_conv_b": nrm(ks[18], (DEPTH, 2 * D_FF), 0.02),
        "w_down": nrm(ks[19], (DEPTH, D_FF, D_MODEL), D_FF ** -0.5),
        "ffn_post_norm": gain(ks[20], D_MODEL),
    }

def reference(x, positions, mix_pre_norm, w_in, attn_sinks, ssd_conv_w, ssd_conv_b, ssd_dt_bias,
              ssd_a_log, ssd_d, ssd_norm, w_attn_out, w_ssd_out, w_out, mix_post_norm,
              ffn_pre_norm, w_up, ffn_conv_w, ffn_conv_b, w_down, ffn_post_norm):
    b, s, _ = x.shape
    h = x
    for l in range(DEPTH):
        u = rmsnorm(h, mix_pre_norm[l])
        proj = u @ w_in[l]
        q, k, v, z, xbc, dt_raw, g_a, g_b = _split(proj, IN_WIDTHS)
        q = rope(q.reshape(b, s, ATTN_HEADS, HEAD_DIM), positions)
        k = rope(k.reshape(b, s, ATTN_KV_HEADS, HEAD_DIM), positions)
        v = v.reshape(b, s, ATTN_KV_HEADS, HEAD_DIM)
        y_attn = banded_sink_attention(q, k, v, attn_sinks[l]) @ w_attn_out[l]
        y_ssd = ssd_mixer(z, xbc, dt_raw, ssd_conv_w[l], ssd_conv_b[l], ssd_dt_bias[l],
                          ssd_a_log[l], ssd_d[l], ssd_norm[l]) @ w_ssd_out[l]
        merged = jax.nn.sigmoid(g_a) * y_attn + jax.nn.sigmoid(g_b) * y_ssd
        h = h + rmsnorm(merged @ w_out[l], mix_post_norm[l])
        f = rmsnorm(h, ffn_pre_norm[l]) @ w_up[l]
        f = causal_dwconv(f, ffn_conv_w[l], ffn_conv_b[l])
        f_gate, f_val = _split(f, (D_FF, D_FF))
        f = (jax.nn.silu(f_gate) * f_val) @ w_down[l]
        h = h + rmsnorm(f, ffn_post_norm[l])
    return h


_drawn_inputs = setup_inputs


def setup_inputs(seed=0):
    import zlib

    import numpy as np

    out = dict(_drawn_inputs(seed))
    spreads = {}
    factors = {'attn_sinks': 8.0, 'ffn_conv_b': 3.464}
    for name, (base, spread) in spreads.items():
        noise = np.random.default_rng([zlib.crc32(name.encode()), seed]).standard_normal(out[name].shape)
        drawn = base * np.exp(spread * noise) if base else spread * noise
        out[name] = __import__('jax').numpy.asarray(drawn.astype(out[name].dtype))
    for name, factor in factors.items():
        out[name] = (out[name] * factor).astype(out[name].dtype)
    return out
```

```python
from contextlib import ExitStack

import concourse.bass as bass
from concourse import mybir

F32 = mybir.dt.float32
F32R = mybir.dt.float32r
I32 = mybir.dt.int32
ALU = mybir.AluOpType
ACT = mybir.ActivationFunctionType
AX_X = mybir.AxisListType.X

P = 128
EPS = 1e-6
ROPE_THETA = 10000.0
MASKED = -1e30
MAGIC = 1.5 * 2.0 ** 23
TWO_PI = (6.28125, 1.9350051879882812e-03, 3.0199159819567529e-07)
PI = 3.1415925


def hybrid_block(nc, x, positions, mix_pre_norm, w_in, attn_sinks, ssd_conv_w, ssd_conv_b, ssd_dt_bias,
                 ssd_a_log, ssd_d, ssd_norm, w_attn_out, w_ssd_out, w_out, mix_post_norm,
                 ffn_pre_norm, w_up, ffn_conv_w, ffn_conv_b, w_down, ffn_post_norm, out):
    S, D = x.shape[1], x.shape[2]
    NT, KD = S // P, D // P
    NG = 4
    HD, QH = 64, 4
    SH = 8
    QW, KW = QH * HD, HD
    XW = SH * HD
    BLK = 2048
    QKV = QW + 2 * KW + SH
    HALF = HD // 2
    INNER, STATE_W = NG * XW, NG * P
    C_K = NG * QW
    C_V = C_K + NG * KW
    C_Z = C_V + NG * KW
    C_X = C_Z + INNER
    C_B = C_X + INNER
    C_C = C_B + STATE_W
    C_DT = C_C + STATE_W
    C_GA = C_DT + NG * SH
    C_GB = C_GA + D
    FF = w_down.shape[1]
    KF = FF // P
    XT = (INNER + 2 * STATE_W) // P
    KI = INNER // P
    TAPS = ssd_conv_w.shape[1]
    FTAPS = ffn_conv_w.shape[1]
    PER_G = 7
    NR1 = KI + KD + 2 * KF + FTAPS * 2 * KF - P
    N_C1 = PER_G * NG
    N_C2 = N_C1 + 2 * NG
    N_D = N_C2 + 3 * NG
    N_E = N_D + KD // 2
    N_F = N_E + KF

    w_in, w_at, w_so = w_in[0], w_attn_out[0], w_ssd_out[0]
    w_o, w_u, w_d = w_out[0], w_up[0], w_down[0]
    x2, out2 = x[0], out[0]

    ctx = ExitStack()
    with ctx:
        def sb(name, shape, dt=F32, where=ctx):
            return where.enter_context(nc.sbuf_tensor(name, shape, dt))

        def sem(name):
            return ctx.enter_context(nc.semaphore(name))

        raw = [sb(f"raw{s}", [P, BLK]) for s in range(2)]
        whi = [sb(f"whi{s}", [P, BLK], F32R) for s in range(2)]
        wlo = [sb(f"wlo{s}", [P, BLK], F32R) for s in range(2)]
        uhi = sb("uhi", [P, KD, S], F32R)
        ulo = sb("ulo", [P, KD, S], F32R)
        oT = sb("oT", [P, KD, S])
        yT = sb("yT", [P, KI, S])
        ident = sb("ident", [P, P])
        par = sb("par", [P, 2, P])
        small = sb("small", [P, 64])
        fcw = sb("fcw", [P, FTAPS + 1, 2 * KF])
        fpar = sb("fpar", [P, 2, FTAPS + 1, 2])
        xin = yT[:, 0:8, :].rearrange("p a b -> p (a b)").rearrange("p (t d) -> p t d", t=NT)
        junk = yT[:, 8:16, :].rearrange("p a b -> p (a b)")

        gctx = ExitStack()
        prow = sb("prow", [P, 3, P], where=gctx)
        posi = sb("posi", [NT, P], I32, where=gctx)
        hp = sb("hp", [P, 3, NG * SH], where=gctx)
        sinks = sb("sinks", [P, NG * QH], where=gctx)
        hpg = sb("hpg", [P, 3, SH], where=gctx)
        sinkg = sb("sinkg", [P, QH], where=gctx)
        cwg = sb("cwg", [P, TAPS + 1, 6], where=gctx)
        inv = sb("inv", [P, HALF], where=gctx)
        cosT = sb("cosT", [P, NT, HALF], where=gctx)
        sinT = sb("sinT", [P, NT, 2, HALF], where=gctx)
        tri = sb("tri", [P, P], where=gctx)
        above_f = sb("above_f", [P, P], where=gctx)
        ones = sb("ones", [P, P], where=gctx)
        above = sb("above", [P, P], F32R, where=gctx)
        qkv_sb = sb("qkv_sb", [P, NT, QKV], where=gctx)
        qk_rot = sb("qk_rot", [P, NT, QW + 2 * KW], where=gctx)
        rtmp = sb("rtmp", [P, QW + KW], where=gctx)
        va = sb("va", [P, NT + 1, HD], where=gctx)
        qT = sb("qT", [P, 2, S], where=gctx)
        kT = sb("kT", [P, S], where=gctx)
        conv = sb("conv", [P, 6, S], where=gctx)
        tanh_c = sb("tanh_c", [P, 2, S], where=gctx)
        b_tok = sb("b_tok", [P, S], where=gctx)
        x_tok = sb("x_tok", [P, NT, XW], where=gctx)
        seg_hi = sb("seg_hi", [P, 2, 512], F32R, where=gctx)
        seg_lo = sb("seg_lo", [P, 2, 512], F32R, where=gctx)
        decay_m = sb("decay_m", [P, SH, P], where=gctx)
        cb_m = sb("cb_m", [P, P], where=gctx)
        probs = sb("probs", [P, QH, P + 1], where=gctx)
        pT = sb("pT", [P, QH, P], where=gctx)
        tanh_z = sb("tanh_z", [P, XW], where=gctx)
        zg = sb("zg", [P, XW], where=gctx)
        xdt = sb("xdt", [P, XW], where=gctx)
        xdtd = sb("xdtd", [P, XW], where=gctx)
        xd = sb("xd", [P, XW], where=gctx)
        yv = sb("yv", [P, XW], where=gctx)
        state = sb("state", [P, XW], where=gctx)
        dtw = sb("dtw", [P, 6, NT * SH], where=gctx)
        dt_s = sb("dt_s", [P, NT, SH], where=gctx)
        adt = sb("adt", [P, NT * SH], where=gctx)
        adt_hi = sb("adt_hi", [P, NT * SH], F32R, where=gctx)
        adt_lo = sb("adt_lo", [P, NT * SH], F32R, where=gctx)
        dec = sb("dec", [P, 3, NT, SH], where=gctx)
        sm = sb("sm", [P, 4, QH], where=gctx)
        gctx.close()

        rhi = sb("rhi", [P, KF, S], F32R)
        rlo = sb("rlo", [P, KF, S], F32R)
        gt = sb("gt", [P, 2, S])
        tga = [gt[:, m, :] for m in range(2)]
        resid = xin
        work = yT[:, 8:16, :]
        normw = oT[:, 0:4, :].rearrange("p a b -> p (a b)").rearrange("p (w d) -> p w d", w=2)

        ps = ctx.enter_context(nc.psum_tensor("ps", [P, 8, 512], F32))

        S_ = {}
        for name in (
            "x_in0", "x_in1", "x_in2", "x_in3", "consts_in", "par_in", "pool_c", "loaded0", "loaded1", "hi_done", "lo_done", "blk_done",
            "act_chain", "dve_chain", "pool_chain", "xsq", "rstd", "xn", "xT_mm", "u_plain", "uhi_ok", "u_ok", "yv_zero", "parT_mm", "par_ok",
            "ang_ok", "rope_tab", "params_ok", "hp_ok",
            "qkv_mm", "qkv_sb", "roped", "va_ok", "dtabs", "dtexp", "dt_ok", "decay_mm", "decay_ok",
            "qkT_mm", "qkT_sb", "conv_mm", "tapped", "conv_ok", "tanhed", "silu_ok", "tok_mm", "tok_sb",
            "seg_hi_ok", "seg_lo_ok", "seg_mm", "lexp", "cb_mm", "cbm_ok", "s_mm", "smx", "sexp", "p_ok", "z_mm", "ztanh", "zg_ok",
            "m_ok", "pT_mm", "pT_sb", "y_mm", "y_done", "xdt_ok", "xdtd_ok", "xd_ok", "st_mm", "st_ok", "w_ok", "wsq",
            "yrstd", "yn_ok", "yT_mm", "yT_sb", "o_mm", "o_sb",
            "split_hi", "split_lo", "ga_mm", "ga_tanh", "at_mm", "at_ok", "gb_mm", "gb_tanh", "so_mm", "so_ok",
            "mg_hi", "mg_lo", "res_in", "out_mm", "d_sq", "d_rstd", "d_h", "h_sq", "h_rstd", "hn_ok", "hT_mm", "h_plain", "h_hi", "h_ok",
            "up_mm", "ftap", "fconv", "ftanh", "f_ok", "fhi_ok", "flo_ok", "fpar_ok", "dn_mm", "e_sq", "e_rstd", "e_ok", "stored",
        ):
            S_[name] = sem(name)
        s = S_
        loaded = [s["loaded0"], s["loaded1"]]
        x_in = [s[f"x_in{t}"] for t in range(NT)]

        block = ctx.enter_context(nc.Block())

        def bank(b, n=512):
            return ps[:, b, 0:n]

        def two(v):
            return v.rearrange("p a b -> p (a b)")

        def plain(t):
            return two(work[:, 2 * t:2 * t + 2, :]).rearrange("p (k c) -> p k c", k=KD)

        def tile_done(eng, G, f):
            if f % 2 == 0:
                eng.wait_ge(s["conv_mm"], G * 3 + (f // 2 + 1))
            else:
                eng.wait_ge(s["blk_done"], G * PER_G + (3 + f // 2))

        TOK_BANK = (0, 1, 1, 7, 1)

        def loaded_by(i, q, per=PER_G):
            return 64 * (i * per + q // 2 + 1)

        @block.sync
        def _(sp):
            for t in range(NT):
                sp.dma_start(xin[:, t, :], x2[t * P:(t + 1) * P, :]).then_inc(x_in[t], 16)
            def put(n, pieces):
                if n >= 2:
                    sp.wait_ge(s["lo_done"], n - 1)
                for dst, src in pieces:
                    sp.dma_start(dst, src).then_inc(loaded[n % 2], 64 // len(pieces))

            def rows_of(w, k0, nk, c0, width):
                return w[k0 * P:(k0 + nk) * P, c0:c0 + width].rearrange("(k p) n -> p k n", p=P)

            for g in range(NG):
                n = PER_G * g
                for h in range(2):
                    v = raw[(n + h) % 2][:, 0:4 * QKV].rearrange("p (k n) -> p k n", k=4)
                    put(n + h, [(v[:, :, 0:QW], rows_of(w_in, 4 * h, 4, g * QW, QW)),
                                (v[:, :, QW:QW + KW], rows_of(w_in, 4 * h, 4, C_K + g * KW, KW)),
                                (v[:, :, QW + KW:QW + 2 * KW], rows_of(w_in, 4 * h, 4, C_V + g * KW, KW)),
                                (v[:, :, QW + 2 * KW:QKV], rows_of(w_in, 4 * h, 4, C_DT + g * SH, SH))])
                v = raw[(n + 2) % 2].rearrange("p (k n) -> p k n", k=KD)
                put(n + 2, [(v[:, :, 0:P], rows_of(w_in, 0, KD, C_B + g * P, P)),
                            (v[:, :, P:2 * P], rows_of(w_in, 0, KD, C_C + g * P, P))])
                for r in range(2):
                    v = raw[(n + 3 + r) % 2].rearrange("p (k n) -> p k n", k=KD)
                    put(n + 3 + r, [(v, rows_of(w_in, 0, KD, C_X + g * XW + 256 * r, 256))])
                for h in range(2):
                    v = raw[(n + 5 + h) % 2].rearrange("p (k n) -> p k n", k=4)
                    put(n + 5 + h, [(v, rows_of(w_in, 4 * h, 4, C_Z + g * XW, XW))])

            def wide(sl):
                return raw[sl].rearrange("p (k n) -> p k n", k=KD)

            for i in range(NG):
                put(N_C1 + 2 * i, [(wide(0), rows_of(w_in, 0, KD, C_GA + 256 * i, 256))])
                put(N_C1 + 2 * i + 1, [(wide(1), rows_of(w_at, 0, KD, 256 * i, 256))])
            for i in range(NG):
                n = N_C2 + 3 * i
                put(n, [(wide(n % 2), rows_of(w_in, 0, KD, C_GB + 256 * i, 256))])
                for h in range(2):
                    put(n + 1 + h, [(wide((n + 1 + h) % 2), rows_of(w_so, h * KD, KD, 256 * i, 256))])
            for b in range(KD // 2):
                put(N_D + b, [(raw[b % 2].rearrange("p (k n) -> p k n", k=2), rows_of(w_o, 2 * b, 2, 0, D))])
                if b == 0:
                    sp.wait_ge(s["split_lo"], KD + KI)
                    sp.dma_start(resid, x2.rearrange("(t p) d -> p t d", p=P)).then_inc(s["res_in"], 16)
                if b == KD // 2 - 1:
                    sp.wait_ge(s["mg_lo"], KD)
                    sp.dma_start(normw[:, 0, :], mix_post_norm[0].partition_broadcast(P)).then_inc(s["res_in"], 16)
                    sp.dma_start(normw[:, 1, :], ffn_post_norm[0].partition_broadcast(P)).then_inc(s["res_in"], 16)
            for j in range(KF):
                put(N_E + j, [(wide(j % 2)[:, :, h * P:(h + 1) * P], rows_of(w_u, 0, KD, FF * h + P * j, P)) for h in range(2)])
            for b in range(KF // 2):
                put(N_F + b, [(raw[b % 2].rearrange("p (k n) -> p k n", k=2), rows_of(w_d, 2 * b, 2, 0, D))])
            for t in range(NT):
                sp.wait_ge(s["e_ok"], t + 1)
                sp.dma_start(out2[t * P:(t + 1) * P, :], work[:, 2 * t:2 * t + 2, :].rearrange("p a b -> p (a b)")).then_inc(s["stored"], 16)
            sp.wait_ge(s["stored"], 16 * NT)

        @block.gpsimd
        def _(pool):
            chain = [0]

            def link(ins):
                chain[0] += 1
                ins.then_inc(s["pool_chain"], 1)
                pool.wait_ge(s["pool_chain"], chain[0])

            for t_, v in ((ident, 0.0), (tri, 1.0), (above_f, 1.0)):
                link(pool.memset(t_[:, :], v))
            link(pool.memset(small[:, 0:1], -0.5))
            link(pool.memset(ones[:, :], 1.0))
            for k in range(HALF):
                f = float(bass_f32_inverse(k, HD))
                pool.memset(inv[:, k:k + 1], f).then_inc(s["pool_c"], 1)
            pool.affine_select(out=ident[:, :], in_=ident[:, :], compare_op=ALU.not_equal, fill=1.0, base=0,
                               pattern=[[-1, P]], channel_multiplier=1).then_inc(s["pool_c"], 1)
            pool.affine_select(out=tri[:, :], in_=tri[:, :], compare_op=ALU.is_ge, fill=0.0, base=0,
                               pattern=[[1, P]], channel_multiplier=-1).then_inc(s["pool_c"], 1)
            pool.affine_select(out=above_f[:, :], in_=above_f[:, :], compare_op=ALU.is_gt, fill=0.0, base=0,
                               pattern=[[-1, P]], channel_multiplier=1).then_inc(s["pool_c"], 1)

            def inverse_root(dst, ssum, scale, done):
                pool.tensor_scalar(dst, ssum, scale, EPS, ALU.mult, ALU.add).then_inc(s["pool_c"], 1)
                count[0] += 1
                pool.wait_ge(s["pool_c"], count[0])
                pool.tensor_tensor(dst, dst, small[:, 0:1], ALU.pow).then_inc(s[done], 1)

            count = [HALF + 3]
            for t in range(NT):
                pool.wait_ge(s["xsq"], t + 1)
                inverse_root(small[:, 8 + t:9 + t], small[:, 4 + t:5 + t], 1.0 / D, "rstd")
            base = count[0]

            def group(i, p):
                G = i * 2 + p
                def build(t):
                    for q in range(2):
                        a = adt_lo[:, t * SH + 4 * q:t * SH + 4 * q + 4].bitcast(F32)
                        pool.tensor_tensor(seg_lo[:, q, :].rearrange("p (h l) -> p h l", h=4),
                                           tri[:, :].unsqueeze(1).to_broadcast([P, 4, P]),
                                           a.unsqueeze(2).to_broadcast([P, 4, P]), ALU.mult).then_inc(s["seg_lo_ok"], 1)

                pool.wait_ge(s["dt_ok"], G + 1)
                pool.wait_ge(s["seg_mm"], G * 2 * NT)
                build(0)
                view = lambda b: b[:, :].rearrange("p (h d) -> p h d", h=SH)
                bc = lambda a: a.unsqueeze(2).to_broadcast([P, SH, HD])
                for t in range(NT):
                    T = G * NT + t
                    if t < NT - 1:
                        pool.wait_ge(s["seg_mm"], T * 2 + 2)
                        build(t + 1)
                    if t == 0:
                        pool.wait_ge(s["decay_ok"], G + 1)
                        pool.wait_ge(s["y_mm"], T)
                    else:
                        pool.wait_ge(s["st_mm"], G * (NT - 1) + t)
                    pool.wait_ge(s["xdt_ok"], T + 1)
                    pool.tensor_tensor(view(xdtd), view(xdt), bc(dec[:, 0, t, :]), ALU.mult).then_inc(s["xdtd_ok"], 1)
                    pool.wait_ge(s["w_ok"], T)
                    pool.tensor_tensor(view(xd), x_tok[:, t, :].rearrange("p (h d) -> p h d", h=SH), bc(hpg[:, 2, :]),
                                       ALU.mult).then_inc(s["xd_ok"], 1)
                    pool.wait_ge(s["pool_c"], HALF + 3)
                    pool.wait_ge(s["wsq"], T + 1)
                    pool.tensor_scalar(small[:, 20:21], small[:, 16:17], 1.0 / (4 * XW), EPS, ALU.mult,
                                       ALU.add).then_inc(s["pool_c"], 1)
                    pool.wait_ge(s["pool_c"], T + (base + 1))
                    pool.wait_ge(s["yn_ok"], T)
                    pool.tensor_tensor(small[:, 17:18], small[:, 20:21], small[:, 0:1], ALU.pow).then_inc(s["yrstd"], 1)

            with pool.Fori(0, NG // 2) as i:
                group(i, 0)
                group(i, 1)
            count[0] = base + NG * NT
            for t in range(NT):
                pool.wait_ge(s["d_sq"], t + 1)
                inverse_root(small[:, 28 + t:29 + t], small[:, 24 + t:25 + t], 1.0 / D, "d_rstd")
                pool.wait_ge(s["h_sq"], t + 1)
                inverse_root(small[:, 36 + t:37 + t], small[:, 32 + t:33 + t], 1.0 / D, "h_rstd")
            for t in range(NT):
                pool.wait_ge(s["e_sq"], t + 1)
                inverse_root(small[:, 44 + t:45 + t], small[:, 40 + t:41 + t], 1.0 / D, "e_rstd")

        @block.scalar
        def _(act):
            def hi(sl, landed, n_next, width=BLK):
                act.wait_ge(loaded[sl], landed)
                if n_next is not None:
                    act.wait_ge(s["blk_done"], n_next)
                act.activation(whi[sl][:, 0:width], raw[sl][:, 0:width], ACT.Copy).then_inc(s["hi_done"], 1)

            for k in range(TAPS):
                act.dma_start(prow[k * XT:(k + 1) * XT, 0, :], ssd_conv_w[0, k].rearrange("(t c) -> t c", c=P)).then_inc(s["par_in"], 16)
            at = TAPS * XT
            for v in (ssd_conv_b[0], mix_pre_norm[0]):
                n = v.shape[0] // P
                act.dma_start(prow[at:at + n, 0, :], v.rearrange("(t c) -> t c", c=P)).then_inc(s["par_in"], 16)
                at += n
            rows = ffn_conv_w[0].rearrange("k (t c) -> (k t) c", c=P)
            act.dma_start(prow[:, 2, :], rows[0:P]).then_inc(s["par_in"], 16)
            at = 0
            for v in (ssd_norm[0], ffn_pre_norm[0], ffn_conv_b[0]):
                n = v.shape[0] // P
                act.dma_start(prow[at:at + n, 1, :], v.rearrange("(t c) -> t c", c=P)).then_inc(s["par_in"], 16)
                at += n
            act.dma_start(prow[at:at + FTAPS * 2 * KF - P, 1, :], rows[P:]).then_inc(s["par_in"], 16)
            act.dma_start(posi[:, :], positions[0].rearrange("(t c) -> t c", c=P)).then_inc(s["par_in"], 16)
            for j, v in enumerate((ssd_dt_bias, ssd_a_log, ssd_d)):
                act.dma_start(hp[:, j, :], v[0].partition_broadcast(P)).then_inc(s["consts_in"], 16)
            act.dma_start(sinks[:, :], attn_sinks[0].partition_broadcast(P)).then_inc(s["consts_in"], 16)

            for t in range(NT):
                act.wait_ge(x_in[t], 16)
                act.activation(junk[:, t * D:(t + 1) * D], xin[:, t, :], ACT.Square,
                               accum_out=small[:, 4 + t:5 + t]).then_inc(s["xsq"], 1)
            act.wait_ge(s["parT_mm"], 4)
            NCP = (TAPS + 1) * XT
            act.activation(par[:, 0, 0:NCP], ps[:, 0, 0:NCP], ACT.Copy, scale=0.5).then_inc(s["par_ok"], 1)
            act.activation(par[:, 0, NCP:P], ps[:, 0, NCP:P], ACT.Copy).then_inc(s["par_ok"], 1)
            act.activation(par[:, 1, 0:NR1], ps[:, 1, 0:NR1], ACT.Copy).then_inc(s["par_ok"], 1)
            act.activation(fcw[:, :, :].rearrange("p k t -> p (k t)")[:, 0:P], ps[:, 2, 0:P], ACT.Copy).then_inc(s["par_ok"], 1)
            act.activation(small[:, 12:16], ps[:, 3, 0:NT], ACT.Copy).then_inc(s["par_ok"], 1)
            act.wait_ge(s["par_ok"], 5)
            for t in range(NT):
                act.wait_ge(s["u_plain"], t + 1)
                act.activation(uhi[:, :, t * P:(t + 1) * P], plain(t), ACT.Copy).then_inc(s["uhi_ok"], 1)
            hi(0, 64, None, 4 * QKV)
            act.wait_ge(s["ang_ok"], 2)
            act.activation(sinT[:, :, 1, :], tanh_c[:, 0, 0:NT * HALF].rearrange("p (t k) -> p t k", t=NT), ACT.Sin).then_inc(s["rope_tab"], 1)
            act.activation(cosT[:, :, :], tanh_c[:, 0, NT * HALF:2 * NT * HALF].rearrange("p (t k) -> p t k", t=NT), ACT.Sin).then_inc(s["rope_tab"], 1)
            act.wait_ge(s["consts_in"], 64)
            act.activation(hp[:, 1, :], hp[:, 1, :], ACT.Exp).then_inc(s["hp_ok"], 1)

            def group(i, p):
                G = i * 2 + p

                def hi_next(j, width=BLK):
                    q = PER_G * p + j + 1
                    hi(q % 2, loaded_by(i, q), G * PER_G + j, width)

                def tap(f):
                    tile_done(act, G, f)
                    act.activation(conv[:, f, :], bank(4 + f % 4), ACT.Identity, scale=cwg[:, TAPS - 1, f:f + 1],
                                   bias=cwg[:, TAPS, f:f + 1]).then_inc(s["tapped"], 1)

                def tanh(f):
                    act.wait_ge(s["conv_ok"], G * 6 + (f + 1))
                    act.activation(tanh_c[:, f % 2, :], conv[:, f, :], ACT.Tanh).then_inc(s["tanhed"], 1)

                def turn_y(t, first_tile, b):
                    act.activation(yT[:, bass.ds(first_tile, 4), t * P:(t + 1) * P],
                                   bank(b).rearrange("p (f c) -> p f c", f=4), ACT.Copy).then_inc(s["yT_sb"], 1)

                def tok(f):
                    act.wait_ge(s["tok_mm"], G * 5 + (f + 1))
                    if f == 0:
                        act.activation(b_tok[:, :], bank(0), ACT.Copy).then_inc(s["tok_sb"], 1)
                    else:
                        act.activation(x_tok[:, :, (f - 1) * P:f * P], bank(TOK_BANK[f]).rearrange("p (t c) -> p t c", t=NT),
                                       ACT.Copy).then_inc(s["tok_sb"], 1)

                def build(t):
                    for h in range(SH):
                        act.activation(seg_hi[:, h // 4, (h % 4) * P:(h % 4 + 1) * P], tri[:, :], ACT.Copy,
                                       scale=adt_hi[:, t * SH + h:t * SH + h + 1].bitcast(F32)).then_inc(s["seg_hi_ok"], 1)

                hi_next(0, 4 * QKV)
                act.wait_ge(s["yT_mm"], G * NT + 1)
                turn_y(NT - 1, i * 8 if p else i * (-8) + 12, 7)
                hi_next(1)
                for t in range(NT):
                    if t < NT - 1:
                        act.wait_ge(s["qkv_mm"], G * (NT - 1) + (t + 1))
                    else:
                        act.wait_ge(s["blk_done"], G * PER_G + 2)
                    if t == 0:
                        act.wait_ge(s["o_mm"], G * NT)
                    vc = slice(QW + KW, QW + 2 * KW)
                    act.activation(va[0:64, t, :], ps[0:64, t, vc], ACT.Copy).then_inc(s["va_ok"], 1)
                    act.activation(va[64:128, t + 1, :], ps[64:128, t, vc], ACT.Copy).then_inc(s["va_ok"], 1)
                    act.activation(qkv_sb[:, t, :], bank(t, QKV), ACT.Copy).then_inc(s["qkv_sb"], 1)
                hi_next(2)
                act.wait_ge(s["params_ok"], G * 5 + 5)
                act.wait_ge(s["y_mm"], G * NT)
                tap(0)
                act.wait_ge(s["dtabs"], G + 1)
                act.activation(dtw[:, 2, :], dtw[:, 1, :], ACT.Exp, scale=-1.0).then_inc(s["dtexp"], 1)
                tap(1)
                tanh(0)
                hi_next(3)
                tap(2)
                tanh(1)
                tap(3)
                act.wait_ge(s["dt_ok"], G + 1)
                act.wait_ge(s["seg_mm"], G * 2 * NT)
                build(0)
                tanh(2)
                hi_next(4)
                tap(4)
                tanh(3)
                tap(5)
                tanh(4)
                hi_next(5)
                for j in range(3):
                    act.wait_ge(s["qkT_mm"], G * 3 + (j + 1))
                    act.activation(qT[:, j, :] if j < 2 else kT[:, :], bank(j), ACT.Copy,
                                   scale=HD ** -0.5 if j < 2 else 1.0).then_inc(s["qkT_sb"], 1)
                act.wait_ge(s["decay_mm"], G + 1)
                act.activation(dec[:, :, :, :].rearrange("p a t h -> p (a t h)"), bank(3, 3 * NT * SH), ACT.Exp).then_inc(s["decay_ok"], 1)
                tanh(5)
                act.wait_ge(s["xd_ok"], G * NT)
                tok(0)
                tok(1)

                for t in range(NT):
                    T = G * NT + t
                    for q in range(2):
                        act.wait_ge(s["seg_mm"], T * 2 + (q + 1))
                        act.wait_ge(s["y_mm"], T)
                        act.activation(decay_m[:, 4 * q:4 * q + 4, :].rearrange("p h l -> p (h l)"), bank(2 + q),
                                       ACT.Exp).then_inc(s["lexp"], 1)

                    def softmax_exp():
                        act.wait_ge(s["smx"], T + 1)
                        pr = probs[:, :, :].rearrange("p h l -> p (h l)")
                        act.activation(pr, pr, ACT.Exp).then_inc(s["sexp"], 1)

                    if t:
                        softmax_exp()
                    if t < NT - 1:
                        act.wait_ge(s["seg_mm"], T * 2 + 2)
                        build(t + 1)
                    if t < NT - 1:
                        act.wait_ge(s["z_mm"], G * (NT - 1) + (t + 1))
                    else:
                        act.wait_ge(s["blk_done"], G * PER_G + PER_G)
                    act.wait_ge(s["zg_ok"], T)
                    act.wait_ge(s["wsq"], T)
                    act.activation(tanh_z[:, :], bank(t % 2), ACT.Tanh, scale=0.5).then_inc(s["ztanh"], 1)
                    if t == 0:
                        tok(2)
                        tok(3)
                        tok(4)
                        softmax_exp()
                    if t == NT - 1:
                        hi_next(6, BLK if p else 4 * QKV)
                    if t:
                        act.wait_ge(s["yT_mm"], G * NT + (t + 1))
                        turn_y(t - 1, G * 4, 3)
                    act.wait_ge(s["pT_mm"], T + 1)
                    act.activation(pT[:, :, :].rearrange("p h l -> p (h l)"), bank(4), ACT.Copy).then_inc(s["pT_sb"], 1)
                    act.wait_ge(s["o_mm"], T + 1)
                    act.activation(oT[:, bass.ds(G * 2, 2), t * P:(t + 1) * P],
                                   bank(4, 2 * P).rearrange("p (f c) -> p f c", f=2), ACT.Copy).then_inc(s["o_sb"], 1)
                    act.wait_ge(s["w_ok"], T + 1)
                    act.activation(tanh_z[:, :], yv[:, :], ACT.Square, accum_out=small[:, 16:17]).then_inc(s["wsq"], 1)

            with act.Fori(0, NG // 2) as i:
                group(i, 0)
                group(i, 1)

            act.wait_ge(s["yT_mm"], NG * NT + 1)
            act.activation(yT[:, KI - 4:KI, (NT - 1) * P:S], bank(7).rearrange("p (f c) -> p f c", f=4), ACT.Copy).then_inc(s["yT_sb"], 1)
            act.wait_ge(s["o_sb"], NG * NT)
            hi(1, 64 * (N_C1 // 2 + 1), N_C1)
            for k in range(KD):
                act.activation(rhi[:, KD + k, :], oT[:, k, :], ACT.Copy).then_inc(s["split_hi"], 1)
            SN = 0
            for k in range(KD):
                act.activation(rhi[:, k, :], yT[:, k, :], ACT.Copy, scale=par[:, 1, SN + k:SN + k + 1]).then_inc(s["split_hi"], 1)

            def gate_a(i, first=False):
                n = i * 2 + N_C1
                if not first:
                    hi(1, 64 * (i + (N_C1 // 2 + 1)), n)
                for m in range(2):
                    if m == 0:
                        act.wait_ge(s["ga_mm"], i + 1)
                    else:
                        act.wait_ge(s["blk_done"], n + 1)
                    act.wait_ge(s["at_ok"], i * 2)
                    act.activation(tga[m], bank(m), ACT.Tanh, scale=0.5).then_inc(s["ga_tanh"], 1)
                hi(0, 64 * (i + (N_C1 // 2 + 2)), n + 1)

            gate_a(0, True)
            with act.Fori(1, NG) as i:
                gate_a(i)
            act.wait_ge(s["at_ok"], 2 * NG)
            act.wait_ge(s["blk_done"], N_C2)
            for k in range(KD, KI):
                act.activation(rhi[:, k, :], yT[:, k, :], ACT.Copy, scale=par[:, 1, SN + k:SN + k + 1]).then_inc(s["split_hi"], 1)
            with act.Fori(0, NG // 2) as i:
                for q in range(6):
                    r, j = divmod(q, 3)
                    n = i * 6 + (N_C2 + q)
                    hi((q + 1) % 2, 64 * (i * 3 + ((N_C2 + q + 1) // 2 + 1)), n)
                    if j == 0:
                        for m in range(2):
                            if m == 0:
                                act.wait_ge(s["gb_mm"], i * 2 + (r + 1))
                            else:
                                act.wait_ge(s["blk_done"], n + 1)
                            act.wait_ge(s["so_ok"], i * 4 + 2 * r)
                            act.activation(tga[m], bank(4 + m), ACT.Tanh, scale=0.5).then_inc(s["gb_tanh"], 1)
            act.wait_ge(s["blk_done"], N_D - 2)
            for k in range(KD):
                act.wait_ge(s["so_ok"], k + 1)
                act.activation(uhi[:, k, :], oT[:, k, :], ACT.Copy, scale=0.5).then_inc(s["mg_hi"], 1)
            def hi_of(n):
                hi(n % 2, 64 * (n // 2 + 1), n - 1)

            def h_hi(t):
                act.wait_ge(s["h_plain"], t + 1)
                act.activation(uhi[:, :, t * P:(t + 1) * P], plain(t), ACT.Copy).then_inc(s["h_hi"], 1)

            for b in range(1, KD // 2):
                hi_of(N_D + b)
            for t in range(NT):
                if t == NT - 1:
                    hi_of(N_E)
                if t < NT - 1:
                    act.wait_ge(s["out_mm"], t + 1)
                else:
                    act.wait_ge(s["blk_done"], N_E)
                act.activation(two(work[:, 2 * t:2 * t + 2, :]), two(ps[:, 2 * t:2 * t + 2, :]), ACT.Square,
                               accum_out=small[:, 24 + t:25 + t]).then_inc(s["d_sq"], 1)
                act.wait_ge(s["d_h"], t + 1)
                act.activation(two(work[:, 2 * t:2 * t + 2, :]), resid[:, t, :], ACT.Square,
                               accum_out=small[:, 32 + t:33 + t]).then_inc(s["h_sq"], 1)
                if t:
                    h_hi(t - 1)
            hi_of(N_E + 1)
            h_hi(NT - 1)

            def up(i):
                for q in range(2):
                    n = i * 2 + (N_E + q)
                    J = i * 2 + q
                    act.wait_ge(s["fpar_ok"], J * 2 + 2)
                    act.wait_ge(s["f_ok"], J)
                    for v in range(2):
                        if v == 0:
                            act.wait_ge(s["up_mm"], J + 1)
                        else:
                            act.wait_ge(s["blk_done"], n + 1)
                        act.activation(work[:, v, :], bank(2 * q + v), ACT.Identity, scale=fpar[:, q, FTAPS - 1, v:v + 1],
                                       bias=fpar[:, q, FTAPS, v:v + 1]).then_inc(s["ftap"], 1)
                    hi(q, 64 * (i + ((N_E + q + 2) // 2 + 1)), n + 1)
                    act.wait_ge(s["fconv"], J + 1)
                    act.activation(work[:, 2, :], work[:, 0, :], ACT.Tanh).then_inc(s["ftanh"], 1)
                    act.wait_ge(s["f_ok"], J + 1)
                    act.activation(rhi[:, bass.ds(J, 1), :], work[:, 3:4, :], ACT.Copy).then_inc(s["fhi_ok"], 1)

            with act.Fori(0, KF // 2) as i:
                up(i)
            for b in range(2, KF // 2):
                hi_of(N_F + b)
            for t in range(NT):
                if t < NT - 1:
                    act.wait_ge(s["dn_mm"], t + 1)
                else:
                    act.wait_ge(s["blk_done"], N_F + KF // 2)
                act.activation(two(work[:, 2 * t:2 * t + 2, :]), two(ps[:, 2 * t:2 * t + 2, :]), ACT.Square,
                               accum_out=small[:, 40 + t:41 + t]).then_inc(s["e_sq"], 1)

        @block.vector
        def _(dve):
            links = {"n": 0, "base": 0}

            def link(ins):
                links["n"] += 1
                ins.then_inc(s["dve_chain"], 1)
                dve.wait_ge(s["dve_chain"], links["base"] + links["n"])

            def lo(sl, done, width=BLK):
                dve.wait_ge(s["hi_done"], done)
                dve.tensor_tensor(wlo[sl][:, 0:width], raw[sl][:, 0:width], whi[sl][:, 0:width].bitcast(F32),
                                  ALU.subtract).then_inc(s["lo_done"], 1)

            def heads(a, n, w):
                return a.unsqueeze(2).to_broadcast([P, n, w])

            dve.wait_ge(s["par_in"], 16 * 12)
            link(dve.tensor_copy(rtmp[0:NT, 0:P], posi[:, :]))
            dve.wait_ge(s["pool_c"], HALF + 3)
            link(dve.tensor_copy(above[:, :], above_f[:, :]))
            link(dve.memset(yv[:, :], 0.0))

            def weigh(t, turned, weight, done):
                dve.wait_ge(s[turned], t + 1)
                dve.tensor_tensor(plain(t), two(ps[:, 2 * t:2 * t + 2, :]).rearrange("p (k c) -> p k c", k=KD),
                                  weight.unsqueeze(2).to_broadcast([P, KD, P]), ALU.mult).then_inc(s[done], 1)

            def rest(t, hi_name, done):
                dve.wait_ge(s[hi_name], t + 1)
                dve.tensor_tensor(ulo[:, :, t * P:(t + 1) * P], plain(t), uhi[:, :, t * P:(t + 1) * P].bitcast(F32),
                                  ALU.subtract).then_inc(s[done], 1)

            for t in range(NT + 2):
                if t < NT:
                    dve.wait_ge(s["rstd"], t + 1)
                    dve.tensor_scalar(xin[:, t, :], xin[:, t, :], small[:, 8 + t:9 + t], None, ALU.mult).then_inc(s["xn"], 1)
                if 1 <= t <= NT:
                    dve.wait_ge(s["par_ok"], 5)
                    weigh(t - 1, "xT_mm", par[:, 0, (TAPS + 1) * XT:(TAPS + 1) * XT + KD], "u_plain")
                if t >= 2:
                    rest(t - 2, "uhi_ok", "u_ok")
            lo(0, 1, 4 * QKV)
            dve.wait_ge(s["par_ok"], 5)
            w0, w1 = tanh_c[:, 0, :], tanh_c[:, 1, :]
            NA = NT * HALF
            r3 = lambda a: a.rearrange("p (t k) -> p t k", t=NT)
            link(dve.tensor_tensor(r3(w0[:, 0:NA]), small[:, 12:16].unsqueeze(2).to_broadcast([P, NT, HALF]),
                                   inv[:, :].unsqueeze(1).to_broadcast([P, NT, HALF]), ALU.mult))
            link(dve.tensor_scalar(w1[:, 0:NA], w0[:, 0:NA], 1.0 / 6.283185307179586, MAGIC, ALU.mult, ALU.add))
            link(dve.tensor_scalar(w1[:, 0:NA], w1[:, 0:NA], -MAGIC, None, ALU.add))
            for c in TWO_PI:
                link(dve.scalar_tensor_tensor(out=w0[:, 0:NA], in0=w1[:, 0:NA], scalar=-c, in1=w0[:, 0:NA],
                                              op0=ALU.mult, op1=ALU.add))
            link(dve.tensor_scalar(w0[:, 0:NA], w0[:, 0:NA], PI, -PI, ALU.min, ALU.max))
            dve.scalar_tensor_tensor(out=w1[:, NA:2 * NA], in0=w0[:, 0:NA], scalar=-1.0, in1=w0[:, 0:NA],
                                     op0=ALU.mult, op1=ALU.max).then_inc(s["ang_ok"], 1)
            dve.wait_ge(s["ang_ok"], 1)
            dve.tensor_scalar(w0[:, NA:2 * NA], w1[:, NA:2 * NA], -1.0, 1.5707963267948966, ALU.mult, ALU.add).then_inc(s["ang_ok"], 1)
            fl = fcw[:, :, :].rearrange("p k t -> p (k t)")
            nb = KI + KD
            link(dve.tensor_copy(fl[:, P:FTAPS * 2 * KF], par[:, 1, nb + 2 * KF:nb + FTAPS * 2 * KF - P + 2 * KF]))
            link(dve.tensor_copy(fl[:, FTAPS * 2 * KF:], par[:, 1, nb:nb + 2 * KF]))
            link(dve.tensor_scalar(fcw[:, :, 0:KF], fcw[:, :, 0:KF], 0.5, None, ALU.mult))
            dve.wait_ge(s["rope_tab"], 2)
            link(dve.tensor_scalar(sinT[:, :, 0, :], sinT[:, :, 1, :], -1.0, None, ALU.mult))
            dve.wait_ge(s["hp_ok"], 1)
            link(dve.tensor_scalar(hp[:, 1, :], hp[:, 1, :], -1.0, None, ALU.mult))
            before = links["n"]

            def group(i, p):
                G = i * 2 + p
                Q0 = PER_G * p

                def lo_next(j, width=BLK):
                    lo((Q0 + j + 1) % 2, G * PER_G + (j + 2), width)

                def taps(f):
                    dve.wait_ge(s["tapped"], G * 6 + (f + 1))
                    for k in range(TAPS - 2, -1, -1):
                        sh = TAPS - 1 - k
                        ins = dve.scalar_tensor_tensor(out=conv[:, f, sh:], in0=ps[:, 4 + f % 4, 0:S - sh],
                                                       scalar=cwg[:, k, f:f + 1], in1=conv[:, f, sh:], op0=ALU.mult, op1=ALU.add)
                        if k:
                            link(ins)
                        else:
                            ins.then_inc(s["conv_ok"], 1)

                def silu(f):
                    dve.wait_ge(s["tanhed"], G * 6 + (f + 1))
                    dve.scalar_tensor_tensor(out=conv[:, f, :], in0=tanh_c[:, f % 2, :], scalar=1.0, in1=conv[:, f, :],
                                             op0=ALU.add, op1=ALU.mult).then_inc(s["silu_ok"], 1)

                dve.wait_ge(s["xd_ok"], G * NT)
                cw = par[:, 0, 0:(TAPS + 1) * XT].rearrange("p (k t) -> p k t", k=TAPS + 1)
                dve.tensor_copy(cwg[:, :, 2:6], cw[:, :, bass.ds(G * 4, 4)]).then_inc(s["params_ok"], 1)
                dve.tensor_copy(cwg[:, :, 0:1], cw[:, :, bass.ds(G + INNER // P, 1)]).then_inc(s["params_ok"], 1)
                dve.tensor_copy(cwg[:, :, 1:2], cw[:, :, bass.ds(G + (INNER + STATE_W) // P, 1)]).then_inc(s["params_ok"], 1)
                dve.tensor_copy(hpg[:, :, :], hp[:, :, bass.ds(G * SH, SH)]).then_inc(s["params_ok"], 1)
                dve.tensor_copy(sinkg[:, :].rearrange("p (a b) -> p a b", a=2),
                                sinks[:, bass.ds(G * QH, QH)].rearrange("p (b a) -> p a b", a=2)).then_inc(s["params_ok"], 1)
                dve.wait_ge(s["params_ok"], G * 5 + 5)
                lo_next(0, 4 * QKV)
                lo_next(1)
                for t in range(NT):
                    dve.wait_ge(s["qkv_sb"], G * NT + (t + 1))
                    if t == 0:
                        dve.wait_ge(s["qkT_mm"], G * 3)
                    src = qkv_sb[:, t, 0:QW + KW].rearrange("p (h r k) -> p h r k", r=2, k=HALF)
                    dst = qk_rot[:, t, 0:QW + KW].rearrange("p (h r k) -> p h r k", r=2, k=HALF)
                    tmp = rtmp[:, :].rearrange("p (h r k) -> p h r k", r=2, k=HALF)
                    cs = cosT[:, t, :].unsqueeze(1).unsqueeze(1).to_broadcast([P, QH + 1, 2, HALF])
                    link(dve.tensor_tensor(dst, src, cs, ALU.mult))
                    for r in range(2):
                        link(dve.tensor_tensor(tmp[:, :, r, :], src[:, :, 1 - r, :],
                                               sinT[:, t, r, :].unsqueeze(1).to_broadcast([P, QH + 1, HALF]), ALU.mult))
                    link(dve.tensor_tensor(qk_rot[:, t, 0:QW + KW], qk_rot[:, t, 0:QW + KW], rtmp[:, :], ALU.add))
                    dve.tensor_copy(qk_rot[:, t, QW + KW:], qk_rot[:, t, QW:QW + KW]).then_inc(s["roped"], 1)
                    if t == 1:
                        lo_next(2)
                b3 = lambda a: a.rearrange("p (t h) -> p t h", t=NT)
                link(dve.tensor_tensor(b3(dtw[:, 0, :]), qkv_sb[:, :, QW + 2 * KW:QKV],
                                       hpg[:, 0, :].unsqueeze(1).to_broadcast([P, NT, SH]), ALU.add))
                dve.scalar_tensor_tensor(out=dtw[:, 1, :], in0=dtw[:, 0, :], scalar=-1.0, in1=dtw[:, 0, :],
                                         op0=ALU.mult, op1=ALU.max).then_inc(s["dtabs"], 1)
                taps(0)
                dve.wait_ge(s["dtexp"], G + 1)
                link(dve.tensor_scalar(dtw[:, 3, :], dtw[:, 2, :], 2.0, None, ALU.add))
                link(dve.reciprocal(dtw[:, 3, :], dtw[:, 3, :]))
                link(dve.tensor_tensor(dtw[:, 4, :], dtw[:, 2, :], dtw[:, 3, :], ALU.mult))
                link(dve.tensor_tensor(dtw[:, 5, :], dtw[:, 4, :], dtw[:, 4, :], ALU.mult))
                link(dve.tensor_scalar(dtw[:, 3, :], dtw[:, 5, :], 1.0 / 17, None, ALU.mult))
                for d in range(15, 1, -2):
                    link(dve.scalar_tensor_tensor(out=dtw[:, 3, :], in0=dtw[:, 3, :], scalar=1.0 / d, in1=dtw[:, 5, :],
                                                  op0=ALU.add, op1=ALU.mult))
                link(dve.scalar_tensor_tensor(out=dtw[:, 3, :], in0=dtw[:, 3, :], scalar=1.0, in1=dtw[:, 4, :],
                                              op0=ALU.add, op1=ALU.mult))
                link(dve.tensor_scalar(dtw[:, 0, :], dtw[:, 0, :], 0.0, None, ALU.max))
                dts = dt_s[:, :, :].rearrange("p t h -> p (t h)")
                link(dve.scalar_tensor_tensor(out=dts, in0=dtw[:, 3, :], scalar=2.0, in1=dtw[:, 0, :], op0=ALU.mult, op1=ALU.add))
                link(dve.tensor_tensor(b3(adt[:, :]), dt_s[:, :, :], hpg[:, 1, :].unsqueeze(1).to_broadcast([P, NT, SH]), ALU.mult))
                link(dve.tensor_copy(adt_hi[:, :], adt[:, :]))
                dve.tensor_tensor(adt_lo[:, :], adt[:, :], adt_hi[:, :].bitcast(F32), ALU.subtract).then_inc(s["dt_ok"], 1)
                taps(1)
                silu(0)
                lo_next(3)
                taps(2)
                silu(1)
                taps(3)
                silu(2)
                lo_next(4)
                taps(4)
                silu(3)
                taps(5)
                silu(4)
                lo_next(5)
                silu(5)

                h8 = lambda b: b.rearrange("p (h d) -> p h d", h=SH)

                def norm_y(T):
                    dve.wait_ge(s["yrstd"], T + 1)
                    dve.tensor_scalar(yv[:, :], yv[:, :], small[:, 17:18], 0.5, ALU.mult, ALU.mult).then_inc(s["yn_ok"], 1)

                for t in range(NT):
                    T = G * NT + t
                    dve.wait_ge(s["cb_mm"], T + 1)
                    dve.tensor_tensor(cb_m[:, :], bank(6, P), tri[:, :], ALU.mult).then_inc(s["cbm_ok"], 1)
                    dve.wait_ge(s["s_mm"], T + 1)
                    sc = ps[:, 4:6, 0:2 * P].rearrange("p a (b k) -> p a b k", b=2)
                    pr = probs[:, :, :].rearrange("p (a b) k -> p a b k", a=2)
                    mx = sm[:, 1, :].rearrange("p (a b) -> p a b", a=2)
                    if t == 0:
                        link(dve.memset(sc[0:64, :, :, 64:P], MASKED))
                    link(dve.tensor_reduce(sm[:, 0, :].rearrange("p (a b) -> p a b", a=2), sc, AX_X, ALU.max))
                    link(dve.tensor_tensor(sm[:, 1, :], sm[:, 0, :], sinkg[:, :], ALU.max))
                    dve.wait_ge(s["pT_mm"], T)
                    link(dve.tensor_tensor(pr[:, :, :, 0:P], sc, mx.unsqueeze(3).to_broadcast([P, 2, 2, P]), ALU.subtract))
                    dve.tensor_tensor(probs[:, :, P:P + 1], sinkg[:, :].unsqueeze(2), sm[:, 1, :].unsqueeze(2),
                                      ALU.subtract).then_inc(s["smx"], 1)
                    if t:
                        norm_y(T - 1)
                    for q in range(2):
                        dve.wait_ge(s["lexp"], T * 2 + (q + 1))
                        if q == 0:
                            dve.wait_ge(s["cbm_ok"], T + 1)
                        m = decay_m[:, 4 * q:4 * q + 4, :]
                        dve.tensor_tensor(m, m, cb_m[:, :].unsqueeze(1).to_broadcast([P, 4, P]), ALU.mult).then_inc(s["m_ok"], 1)
                    dve.wait_ge(s["y_mm"], T)
                    if t == 0:
                        dve.wait_ge(s["tok_sb"], G * 5 + 5)
                    dve.tensor_tensor(h8(xdt[:, :]), h8(x_tok[:, t, :]), heads(dt_s[:, t, :], SH, HD), ALU.mult).then_inc(s["xdt_ok"], 1)
                    dve.wait_ge(s["sexp"], T + 1)
                    link(dve.tensor_reduce(sm[:, 2, :], probs[:, :, :], AX_X, ALU.add))
                    link(dve.reciprocal(sm[:, 3, :], sm[:, 2, :]))
                    dve.tensor_tensor(probs[:, :, 0:P], probs[:, :, 0:P], heads(sm[:, 3, :], QH, P), ALU.mult).then_inc(s["p_ok"], 1)
                    dve.wait_ge(s["ztanh"], T + 1)
                    dve.scalar_tensor_tensor(out=zg[:, :], in0=tanh_z[:, :], scalar=1.0, in1=bank(t % 2),
                                             op0=ALU.add, op1=ALU.mult).then_inc(s["zg_ok"], 1)
                    if t == NT - 1:
                        lo_next(6, BLK if p else 4 * QKV)
                    dve.wait_ge(s["y_mm"], T + 1)
                    dve.wait_ge(s["xd_ok"], T + 1)
                    if t:
                        link(dve.tensor_tensor(h8(yv[:, :]), h8(bank(6)), heads(dec[:, 1, t, :], SH, HD), ALU.mult))
                        dve.tensor_tensor(yv[:, :], yv[:, :], bank(5), ALU.add).then_inc(s["y_done"], 1)
                        dve.wait_ge(s["y_done"], T + 1)
                        link(dve.tensor_tensor(yv[:, :], yv[:, :], xd[:, :], ALU.add))
                    else:
                        dve.wait_ge(s["yT_mm"], G * NT + 1)
                        dve.tensor_tensor(yv[:, :], bank(5), xd[:, :], ALU.add).then_inc(s["y_done"], 1)
                        dve.wait_ge(s["y_done"], T + 1)
                    dve.wait_ge(s["zg_ok"], T + 1)
                    dve.tensor_tensor(yv[:, :], yv[:, :], zg[:, :], ALU.mult).then_inc(s["w_ok"], 1)
                    if t < NT - 1:
                        dve.wait_ge(s["st_mm"], G * (NT - 1) + (t + 1))
                        if t == 0:
                            dve.tensor_copy(state[:, :], bank(7)).then_inc(s["st_ok"], 1)
                        else:
                            link(dve.tensor_tensor(h8(state[:, :]), h8(state[:, :]), heads(dec[:, 2, t, :], SH, HD), ALU.mult))
                            dve.tensor_tensor(state[:, :], state[:, :], bank(7), ALU.add).then_inc(s["st_ok"], 1)
                norm_y(G * NT + (NT - 1))

            with dve.Fori(0, NG // 2) as i:
                links["n"], links["base"] = 0, i * PAIR_LINKS + before
                group(i, 0)
                group(i, 1)
                assert links["n"] == PAIR_LINKS, links
            links["n"], links["base"] = before + PAIR_LINKS * (NG // 2), 0

            lo(1, N_C1 + 2)
            for k in range(KD):
                dve.wait_ge(s["split_hi"], k + 1)
                dve.tensor_tensor(rlo[:, KD + k, :], oT[:, k, :], rhi[:, KD + k, :].bitcast(F32), ALU.subtract).then_inc(s["split_lo"], 1)

            def split_y(k, count):
                dve.wait_ge(s["split_hi"], count)
                dve.scalar_tensor_tensor(out=rlo[:, k, :], in0=yT[:, k, :], scalar=par[:, 1, k:k + 1],
                                         in1=rhi[:, k, :].bitcast(F32), op0=ALU.mult, op1=ALU.subtract).then_inc(s["split_lo"], 1)

            for k in range(KD):
                split_y(k, KD + k + 1)

            def gate_a(i, first=False):
                n = i * 2 + N_C1
                if not first:
                    lo(1, n + 2)
                lo(0, n + 3)
                for m in range(2):
                    dve.wait_ge(s["ga_tanh"], i * 2 + (m + 1))
                    if m == 0:
                        dve.wait_ge(s["at_mm"], i + 1)
                    else:
                        dve.wait_ge(s["blk_done"], n + 2)
                    dve.scalar_tensor_tensor(out=oT[:, bass.ds(i * 2 + m, 1), :], in0=gt[:, m:m + 1, :], scalar=1.0,
                                             in1=ps[:, 2 + m:3 + m, :], op0=ALU.add, op1=ALU.mult).then_inc(s["at_ok"], 1)

            gate_a(0, True)
            with dve.Fori(1, NG) as i:
                gate_a(i)
            for k in range(KD, KI):
                split_y(k, KD + k + 1)
            before = links["n"]
            with dve.Fori(0, NG // 2) as i:
                links["n"], links["base"] = 0, i * 4 + before
                for q in range(6):
                    r, j = divmod(q, 3)
                    n = i * 6 + (N_C2 + q)
                    lo((q + 1) % 2, n + 2)
                    if j == 2:
                        for m in range(2):
                            dve.wait_ge(s["gb_tanh"], i * 4 + (2 * r + m + 1))
                            if m == 0:
                                dve.wait_ge(s["so_mm"], i * 2 + (r + 1))
                            else:
                                dve.wait_ge(s["blk_done"], n + 1)
                            link(dve.scalar_tensor_tensor(out=tga[m], in0=tga[m], scalar=1.0, in1=bank(6 + m),
                                                          op0=ALU.add, op1=ALU.mult))
                            o_ = oT[:, bass.ds(i * 4 + (2 * r + m), 1), :]
                            dve.tensor_tensor(o_, o_, gt[:, m:m + 1, :], ALU.add).then_inc(s["so_ok"], 1)
            links["n"], links["base"] = before + 4 * (NG // 2), 0
            for k in range(KD):
                dve.wait_ge(s["mg_hi"], k + 1)
                dve.scalar_tensor_tensor(out=ulo[:, k, :], in0=oT[:, k, :], scalar=0.5, in1=uhi[:, k, :].bitcast(F32),
                                         op0=ALU.mult, op1=ALU.subtract).then_inc(s["mg_lo"], 1)
            for b in range(1, KD // 2):
                lo((N_D + b) % 2, N_D + b + 1)
            dve.wait_ge(s["res_in"], 48)

            def norm_h(t):
                dve.wait_ge(s["h_rstd"], t + 1)
                dve.tensor_scalar(two(work[:, 2 * t:2 * t + 2, :]), resid[:, t, :], small[:, 36 + t:37 + t], None,
                                  ALU.mult).then_inc(s["hn_ok"], 1)

            for t in range(NT):
                if t == NT - 1:
                    lo(N_E % 2, N_E + 1)
                dve.wait_ge(s["d_rstd"], t + 1)
                wt = two(work[:, 2 * t:2 * t + 2, :])
                link(dve.scalar_tensor_tensor(out=wt, in0=two(ps[:, 2 * t:2 * t + 2, :]), scalar=small[:, 28 + t:29 + t],
                                              in1=normw[:, 0, :], op0=ALU.mult, op1=ALU.mult))
                dve.tensor_tensor(resid[:, t, :], resid[:, t, :], wt, ALU.add).then_inc(s["d_h"], 1)
                if t:
                    weigh(t - 1, "hT_mm", par[:, 1, KI:KI + KD], "h_plain")
                norm_h(t)
                if t:
                    rest(t - 1, "h_hi", "h_ok")
            lo((N_E + 1) % 2, N_E + 2)
            weigh(NT - 1, "hT_mm", par[:, 1, KI:KI + KD], "h_plain")
            rest(NT - 1, "h_hi", "h_ok")
            before = links["n"]
            UP_LINKS = 2 * 4

            def up(i):
                links["n"], links["base"] = 0, i * UP_LINKS + before
                for q in range(2):
                    J = i * 2 + q
                    n = J + N_E
                    for v in range(2):
                        dve.tensor_copy(fpar[:, q, :, v:v + 1], fcw[:, :, bass.ds(J + KF * v, 1)]).then_inc(s["fpar_ok"], 1)
                    for v in range(2):
                        dve.wait_ge(s["ftap"], J * 2 + (v + 1))
                        for k in range(FTAPS - 2, -1, -1):
                            sh = FTAPS - 1 - k
                            ins = dve.scalar_tensor_tensor(out=work[:, v, sh:], in0=ps[:, 2 * q + v, 0:S - sh],
                                                           scalar=fpar[:, q, k, v:v + 1], in1=work[:, v, sh:], op0=ALU.mult, op1=ALU.add)
                            if k == 0 and v == 0:
                                ins.then_inc(s["fconv"], 1)
                            else:
                                link(ins)
                    dve.wait_ge(s["ftanh"], J + 1)
                    link(dve.scalar_tensor_tensor(out=work[:, 2, :], in0=work[:, 2, :], scalar=1.0, in1=work[:, 0, :],
                                                  op0=ALU.add, op1=ALU.mult))
                    dve.wait_ge(s["flo_ok"], J)
                    dve.tensor_tensor(work[:, 3, :], work[:, 2, :], work[:, 1, :], ALU.mult).then_inc(s["f_ok"], 1)
                    dve.wait_ge(s["fhi_ok"], J + 1)
                    dve.tensor_tensor(rlo[:, bass.ds(J, 1), :], work[:, 3:4, :], rhi[:, bass.ds(J, 1), :].bitcast(F32),
                                      ALU.subtract).then_inc(s["flo_ok"], 1)
                    lo(q, n + 3)
                assert links["n"] == UP_LINKS, links

            with dve.Fori(0, KF // 2) as i:
                up(i)
            links["n"], links["base"] = before + UP_LINKS * (KF // 2), 0
            for b in range(2, KF // 2):
                lo((N_F + b) % 2, N_F + b + 1)
            for t in range(NT):
                dve.wait_ge(s["e_rstd"], t + 1)
                wt = two(work[:, 2 * t:2 * t + 2, :])
                link(dve.scalar_tensor_tensor(out=wt, in0=two(ps[:, 2 * t:2 * t + 2, :]), scalar=small[:, 44 + t:45 + t],
                                              in1=normw[:, 1, :], op0=ALU.mult, op1=ALU.mult))
                dve.tensor_tensor(wt, wt, resid[:, t, :], ALU.add).then_inc(s["e_ok"], 1)

        @block.tensor
        def _(pe):
            def tiles(w, k):
                return w.rearrange("p (k n) -> p k n", k=k)

            def features(b, sl, m, acts, first=True, last=True, span=slice(0, S)):
                hi_, lo_ = tiles(whi[sl][:, :], KD), tiles(wlo[sl][:, :], KD)
                for k in range(KD):
                    ah, al = acts(k)
                    c = slice(m * P, (m + 1) * P)
                    pe.matmul(bank(b)[:, span], hi_[:, k, c], ah[:, span], start=first and k == 0, stop=False)
                    pe.matmul(bank(b)[:, span], hi_[:, k, c], al[:, span], start=False, stop=False)
                    ins = pe.matmul(bank(b)[:, span], lo_[:, k, c], ah[:, span], start=False, stop=last and k == KD - 1)
                return ins

            def tokens(o, ah, al, wh, wl, first, last):
                pe.matmul(o, ah, wh, start=first, stop=False)
                pe.matmul(o, al, wh, start=False, stop=False)
                return pe.matmul(o, ah, wl, start=False, stop=last)

            def u(k):
                return uhi[:, k, :], ulo[:, k, :]

            pe.wait_ge(s["pool_c"], HALF + 1)
            pe.wait_ge(s["par_in"], 16 * 12)
            pe.transpose(ps[:, 0, 0:P], prow[:, 0, :], ident[:, :]).then_inc(s["parT_mm"], 1)
            pe.transpose(ps[:, 1, 0:NR1], prow[0:NR1, 1, :], ident[0:NR1, 0:NR1]).then_inc(s["parT_mm"], 1)
            pe.transpose(ps[:, 2, 0:P], prow[:, 2, :], ident[:, :]).then_inc(s["parT_mm"], 1)
            pe.wait_ge(s["dve_chain"], 1)
            pe.transpose(ps[:, 3, 0:NT], rtmp[0:NT, 0:P], ident[0:NT, 0:NT]).then_inc(s["parT_mm"], 1)
            pe.wait_ge(s["par_ok"], 5)

            def turn_tile(t, src, done):
                for k in range(KD):
                    ins = pe.transpose(ps[:, 2 * t + k // 4, (k % 4) * P:(k % 4 + 1) * P], src[:, k * P:(k + 1) * P], ident[:, :])
                ins.then_inc(s[done], 1)

            for t in range(NT):
                pe.wait_ge(s["xn"], t + 1)
                turn_tile(t, xin[:, t, :], "xT_mm")
            pe.wait_ge(s["dve_chain"], 3)

            def turn_y(b):
                for f in range(4):
                    ins = pe.transpose(ps[:, b, f * P:(f + 1) * P], yv[:, f * P:(f + 1) * P], ident[:, :])
                ins.then_inc(s["yT_mm"], 1)

            def group(i, p):
                G = i * 2 + p
                Q0 = PER_G * p

                def block_ready(j):
                    pe.wait_ge(s["lo_done"], G * PER_G + (j + 1))
                    return (Q0 + j) % 2

                pe.wait_ge(s["zg_ok"], G * NT)
                pe.wait_ge(s["o_sb"], G * NT)
                pe.wait_ge(s["yT_sb"], G * NT)
                for h in range(2):
                    sl = block_ready(h)
                    wh, wl = (w[sl][:, 0:4 * QKV].rearrange("p (k n) -> p k n", k=4) for w in (whi, wlo))
                    for t in range(NT):
                        c = slice(t * P, (t + 1) * P)
                        pe.wait_ge(s["u_ok"], t + 1)
                        for k in range(4):
                            ins = tokens(bank(t, QKV), uhi[:, 4 * h + k, c], ulo[:, 4 * h + k, c], wh[:, k, :], wl[:, k, :],
                                         h == 0 and k == 0, h == 1 and k == 3)
                        if t == NT - 1:
                            ins.then_inc(s["blk_done"], 1)
                        elif h == 1:
                            ins.then_inc(s["qkv_mm"], 1)
                    if h == 0:
                        pe.wait_ge(s["yn_ok"], G * NT)
                        pe.wait_ge(s["st_ok"], G * (NT - 1))
                        turn_y(7)

                def conv_tiles(j):
                    sl = block_ready(j)
                    for m in range(2):
                        f = 2 * (j - 2) + m
                        if f == 0:
                            pe.wait_ge(s["o_sb"], G * NT)
                        elif f == 1:
                            pe.wait_ge(s["y_done"], G * NT)
                        elif f == 3:
                            pe.wait_ge(s["yT_sb"], G * NT + 1)
                        elif f >= 4:
                            pe.wait_ge(s["conv_ok"], G * 6 + (f - 3))
                        features(4 + f % 4, sl, m, u).then_inc(s["conv_mm"] if m == 0 else s["blk_done"], 1)

                conv_tiles(2)
                conv_tiles(3)
                conv_tiles(4)
                pe.wait_ge(s["qkv_sb"], G * NT + NT)
                pe.wait_ge(s["roped"], G * NT + NT)
                for j in range(3):
                    for t in range(NT):
                        ins = pe.transpose(ps[:, j, t * P:(t + 1) * P], qk_rot[:, t, j * P:(j + 1) * P], ident[:, :])
                    ins.then_inc(s["qkT_mm"], 1)
                pe.wait_ge(s["dt_ok"], G + 1)
                for j, m in enumerate((above_f, tri, ones)):
                    ins = pe.matmul(ps[:, 3, j * NT * SH:(j + 1) * NT * SH], m[:, :], adt[:, :], start=True, stop=True)
                ins.then_inc(s["decay_mm"], 1)

                def tok(f):
                    pe.wait_ge(s["silu_ok"], G * 6 + (1 if f == 0 else f + 2))
                    if f < 2:
                        pe.wait_ge(s["qkT_sb"], G * 3 + (f + 1))
                    elif f == 3:
                        pe.wait_ge(s["conv_ok"], G * 6 + 4)
                    else:
                        pe.wait_ge(s["tok_sb"], G * 5 + (f if f == 2 else 3))
                    for t in range(NT):
                        ins = pe.transpose(ps[:, TOK_BANK[f], t * P:(t + 1) * P], conv[:, f + (f > 0), t * P:(t + 1) * P], ident[:, :])
                    ins.then_inc(s["tok_mm"], 1)

                tok(0)
                tok(1)

                for t in range(NT):
                    T = G * NT + t
                    c = slice(t * P, (t + 1) * P)
                    if t == 0:
                        pe.wait_ge(s["qkT_sb"], G * 3 + 3)
                        pe.wait_ge(s["decay_ok"], G + 1)
                    else:
                        pe.wait_ge(s["lexp"], T * 2)
                        pe.wait_ge(s["yT_sb"], G * NT + t)
                    for q in range(2):
                        pe.wait_ge(s["seg_hi_ok"], T * SH + 4 * (q + 1))
                        pe.wait_ge(s["seg_lo_ok"], T * 2 + (q + 1))
                        pe.matmul(bank(2 + q), above[:, :], seg_hi[:, q, :], start=True, stop=False)
                        pe.matmul(bank(2 + q), above[:, :], seg_lo[:, q, :], start=False, stop=True).then_inc(s["seg_mm"], 1)
                    pe.wait_ge(s["silu_ok"], G * 6 + 2)
                    if t == 0:
                        pe.wait_ge(s["conv_ok"], G * 6 + 3)
                    else:
                        pe.wait_ge(s["y_done"], T)
                    pe.matmul(bank(6, P), conv[:, 0, c], conv[:, 1, c], start=True, stop=True).then_inc(s["cb_mm"], 1)
                    def scores():
                        pe.wait_ge(s["qkT_sb"], G * 3 + 3)
                        if t:
                            pe.wait_ge(s["o_sb"], T)
                        else:
                            pe.wait_ge(s["conv_ok"], G * 6 + 6)
                        for h in range(QH):
                            r = slice((h % 2) * 64, (h % 2) * 64 + 64)
                            b, o = 4 + h % 2, (h // 2) * P
                            ins = pe.matmul(ps[:, b, o:o + P], qT[r, h // 2, c], kT[r, c], start=True, stop=True)
                            if t:
                                ins = pe.matmul(ps[0:64, b, o + 64:o + P], qT[r, h // 2, t * P:t * P + 64],
                                                kT[r, t * P - 64:t * P], start=True, stop=True)
                        ins.then_inc(s["s_mm"], 1)

                    def z_tile():
                        zb = t % 2
                        if t == 0:
                            pe.wait_ge(s["tok_sb"], G * 5 + 1)
                        elif t == 1:
                            pe.wait_ge(s["tok_sb"], G * 5 + 5)
                        else:
                            pe.wait_ge(s["zg_ok"], T - 1)
                        for h in range(2):
                            sl = block_ready(5 + h)
                            wh, wl = tiles(whi[sl][:, :], 4), tiles(wlo[sl][:, :], 4)
                            for k in range(4):
                                ins = tokens(bank(zb), uhi[:, 4 * h + k, c], ulo[:, 4 * h + k, c], wh[:, k, :], wl[:, k, :],
                                             h == 0 and k == 0, h == 1 and k == 3)
                            if t == NT - 1:
                                ins.then_inc(s["blk_done"], 1)
                        if t < NT - 1:
                            ins.then_inc(s["z_mm"], 1)

                    if t == 0:
                        z_tile()
                        scores()
                        for f in range(2, 5):
                            tok(f)
                    else:
                        scores()
                        z_tile()
                        pe.wait_ge(s["lexp"], T * 2 + 2)
                        pe.wait_ge(s["yn_ok"], T)
                        turn_y(3)
                    pe.wait_ge(s["m_ok"], T * 2 + 2)
                    pe.wait_ge(s["xdt_ok"], T + 1)
                    if t:
                        pe.wait_ge(s["st_ok"], G * (NT - 1) + t)
                        pe.matmul(bank(6), conv[:, 1, c], state[:, :], start=True, stop=True)
                    pe.wait_ge(s["smx"], T + 1)
                    for h in range(SH):
                        w = P if h < SH - 1 else HD
                        ins = pe.matmul(ps[:, 5, h * HD:h * HD + w], decay_m[:, h, :], xdt[:, h * HD:h * HD + w], start=True, stop=True)
                    ins.then_inc(s["y_mm"], 1)
                    pe.wait_ge(s["p_ok"], T + 1)
                    for h in range(QH):
                        ins = pe.transpose(ps[:, 4, h * P:(h + 1) * P], probs[:, h, 0:P], ident[:, :])
                    ins.then_inc(s["pT_mm"], 1)
                    if t < NT - 1:
                        pe.wait_ge(s["xdtd_ok"], T + 1)
                        if t:
                            pe.wait_ge(s["st_ok"], G * (NT - 1) + t)
                        else:
                            pe.wait_ge(s["tok_sb"], G * 5 + 5)
                        pe.matmul(bank(7), b_tok[:, c], xdtd[:, :], start=True, stop=True).then_inc(s["st_mm"], 1)
                    pe.wait_ge(s["pT_sb"], T + 1)
                    pe.wait_ge(s["va_ok"], T * 2 + 2)
                    for h in range(QH):
                        r = slice((h % 2) * 64, (h % 2) * 64 + 64)
                        for half in (1, 0):
                            o = ps[r, 4, (h // 2) * P + 64 * half:(h // 2) * P + 64 * half + 64]
                            n = 64 if t == 0 and half == 0 else P
                            v = qkv_sb[0:n, t, QW + KW:QW + 2 * KW] if half else va[0:n, t, :]
                            ins = pe.matmul(o, v, pT[0:n, (h % 2) * 2 + h // 2, 64 * half:64 * half + 64], start=True, stop=True)
                    ins.then_inc(s["o_mm"], 1)

            with pe.Fori(0, NG // 2) as i:
                group(i, 0)
                group(i, 1)

            pe.wait_ge(s["zg_ok"], NG * NT)
            pe.wait_ge(s["lexp"], 2 * NG * NT)
            pe.wait_ge(s["yT_sb"], NG * NT)

            def gate_a(i, first=False):
                n = i * 2 + N_C1
                pe.wait_ge(s["lo_done"], n + 1)
                pe.wait_ge(s["ga_tanh"], i * 2)
                features(0, 0, 0, u).then_inc(s["ga_mm"], 1)
                features(1, 0, 1, u).then_inc(s["blk_done"], 1)
                if first:
                    pe.wait_ge(s["yn_ok"], NG * NT)
                    pe.wait_ge(s["st_ok"], NG * (NT - 1))
                    turn_y(7)
                pe.wait_ge(s["lo_done"], n + 2)
                pe.wait_ge(s["split_lo"], KD)
                pe.wait_ge(s["at_ok"], i * 2)
                o = lambda k: (rhi[:, KD + k, :], rlo[:, KD + k, :])
                features(2, 1, 0, o).then_inc(s["at_mm"], 1)
                features(3, 1, 1, o).then_inc(s["blk_done"], 1)

            gate_a(0, True)
            with pe.Fori(1, NG) as i:
                gate_a(i)
            pe.wait_ge(s["o_sb"], NG * NT)
            pe.wait_ge(s["y_done"], NG * NT)
            pe.wait_ge(s["yT_sb"], NG * NT + 1)
            with pe.Fori(0, NG // 2) as i:
                for q in range(6):
                    r, j = divmod(q, 3)
                    pe.wait_ge(s["lo_done"], i * 6 + (N_C2 + q + 1))
                    if j == 0:
                        pe.wait_ge(s["gb_tanh"], i * 4 + 2 * r)
                        features(4, q % 2, 0, u).then_inc(s["gb_mm"], 1)
                        features(5, q % 2, 1, u).then_inc(s["blk_done"], 1)
                    elif j == 1:
                        pe.wait_ge(s["so_ok"], i * 4 + 2 * r)
                        y = lambda k: (rhi[:, k, :], rlo[:, k, :])
                        features(6, q % 2, 0, y, True, False)
                        features(7, q % 2, 1, y, True, False).then_inc(s["blk_done"], 1)
                    else:
                        pe.wait_ge(s["split_lo"], KD + KI)
                        y = lambda k: (rhi[:, KD + k, :], rlo[:, KD + k, :])
                        features(6, q % 2, 0, y, False, True).then_inc(s["so_mm"], 1)
                        features(7, q % 2, 1, y, False, True).then_inc(s["blk_done"], 1)

            def all_tokens(n, n0, acts_hi, acts_lo, tile_ok, bank_ok, done, between=lambda t, b: None):
                def part(b, k, t):
                    wh, wl = tiles(whi[b % 2][:, :], 2), tiles(wlo[b % 2][:, :], 2)
                    c = slice(t * P, (t + 1) * P)
                    for h in range(2):
                        if b == 0 and k == 0:
                            bank_ok(2 * t + h)
                        ins = tokens(bank(2 * t + h), acts_hi[:, 2 * b + k, c], acts_lo[:, 2 * b + k, c],
                                     wh[:, k, 512 * h:512 * h + 512], wl[:, k, 512 * h:512 * h + 512],
                                     b == 0 and k == 0, b == n - 1 and k == 1)
                    return ins

                def ready(b):
                    pe.wait_ge(s["lo_done"], n0 + b + 1)
                    tile_ok(2 * b + 2)

                for b in range(n - 2):
                    ready(b)
                    for k in range(2):
                        for t in order:
                            ins = part(b, k, t)
                    ins.then_inc(s["blk_done"], 1)
                for t in range(NT):
                    for b in (n - 2, n - 1):
                        if t == 0:
                            ready(b)
                        for k in range(2):
                            ins = part(b, k, t)
                        if t == NT - 1:
                            ins.then_inc(s["blk_done"], 1)
                        elif b == n - 1:
                            ins.then_inc(s[done], 1)
                        between(t, b)

            def bank_ok(b):
                if b >= 6:
                    pe.wait_ge(s["so_ok"], KD)

            order = range(NT)

            def turn_h(t):
                pe.wait_ge(s["hn_ok"], t + 1)
                turn_tile(t, two(work[:, 2 * t:2 * t + 2, :]), "hT_mm")

            def between(t, b):
                if (t, b) == (NT - 2, KD // 2 - 1):
                    turn_h(0)
                if (t, b) == (NT - 1, KD // 2 - 2):
                    turn_h(1)

            all_tokens(KD // 2, N_D, uhi, ulo, lambda k: pe.wait_ge(s["mg_lo"], k), bank_ok, "out_mm", between)

            half = slice(0, S // 2), slice(S // 2, S)
            for q in range(2):
                pe.wait_ge(s["lo_done"], N_E + q + 1)
                pe.wait_ge(s["h_ok"], NT // 2)
                for m in range(2):
                    features(2 * q + m, q, m, u, span=half[0])
                turn_h(NT // 2 + q)
            for q in range(2):
                pe.wait_ge(s["h_ok"], NT)
                features(2 * q, q, 0, u, span=half[1]).then_inc(s["up_mm"], 1)
                features(2 * q + 1, q, 1, u, span=half[1]).then_inc(s["blk_done"], 1)

            def up(i):
                for q in range(2):
                    J = i * 2 + q
                    pe.wait_ge(s["lo_done"], J + (N_E + 1))
                    pe.wait_ge(s["f_ok"], J - 1)
                    features(2 * q, q, 0, u).then_inc(s["up_mm"], 1)
                    features(2 * q + 1, q, 1, u).then_inc(s["blk_done"], 1)

            with pe.Fori(1, KF // 2) as i:
                up(i)
            order = (3, 2, 0, 1)

            def bank_ok(b):
                if b < 4:
                    pe.wait_ge(s["f_ok"], KF - 1 + b // 2)

            all_tokens(KF // 2, N_F, rhi, rlo, lambda k: pe.wait_ge(s["flo_ok"], k), bank_ok, "dn_mm")


def bass_f32_inverse(k, width):
    import numpy as np
    return np.float32(1.0) / np.float32(ROPE_THETA ** (2.0 * k / width))


PAIR_LINKS = 150

_INS = ['x', 'positions', 'mix_pre_norm', 'w_in', 'attn_sinks', 'ssd_conv_w', 'ssd_conv_b', 'ssd_dt_bias',
        'ssd_a_log', 'ssd_d', 'ssd_norm', 'w_attn_out', 'w_ssd_out', 'w_out', 'mix_post_norm',
        'ffn_pre_norm', 'w_up', 'ffn_conv_w', 'ffn_conv_b', 'w_down', 'ffn_post_norm']


def kernel(**inputs):
    import numpy as _np
    import concourse.bacc as _bacc
    from concourse import mybir as _mybir
    from concourse.bass_utils import run_bass_kernel_spmd as _run

    nc = _bacc.Bacc("TRN2", target_bir_lowering=False, num_devices=1, dynamic_dma_scratch_size=1024)
    arrays, args = {}, []
    for name in _INS:
        a = _np.ascontiguousarray(inputs[name])
        arrays[f"in_{name}_dram"] = a
        args.append(nc.dram_tensor(f"in_{name}_dram", a.shape, _mybir.dt.from_np(a.dtype), kind="ExternalInput").ap())
    shape = tuple(inputs["x"].shape)
    args.append(nc.dram_tensor("out_0_dram", shape, _mybir.dt.float32, kind="ExternalOutput").ap())
    hybrid_block(nc, *args)
    r = _run(nc, [arrays], core_ids=[0])
    return r.results[0]["out_0_dram"]
```

```python
from contextlib import ExitStack

import concourse.bass as bass
from concourse import mybir

F32 = mybir.dt.float32
F32R = mybir.dt.float32r
I32 = mybir.dt.int32
ALU = mybir.AluOpType
ACT = mybir.ActivationFunctionType
AX_X = mybir.AxisListType.X

P = 128
EPS = 1e-6
ROPE_THETA = 10000.0
MASKED = -1e30
MAGIC = 1.5 * 2.0 ** 23
TWO_PI = (6.28125, 1.9350051879882812e-03, 3.0199159819567529e-07)
PI = 3.1415925


def hybrid_block(nc, x, positions, mix_pre_norm, w_in, attn_sinks, ssd_conv_w, ssd_conv_b, ssd_dt_bias,
                 ssd_a_log, ssd_d, ssd_norm, w_attn_out, w_ssd_out, w_out, mix_post_norm,
                 ffn_pre_norm, w_up, ffn_conv_w, ffn_conv_b, w_down, ffn_post_norm, out):
    S, D = x.shape[1], x.shape[2]
    NT, KD = S // P, D // P
    NG = 4
    HD, QH = 64, 4
    SH = 8
    QW, KW = QH * HD, HD
    XW = SH * HD
    BLK = 2048
    QKV = QW + 2 * KW + SH
    HALF = HD // 2
    INNER, STATE_W = NG * XW, NG * P
    C_K = NG * QW
    C_V = C_K + NG * KW
    C_Z = C_V + NG * KW
    C_X = C_Z + INNER
    C_B = C_X + INNER
    C_C = C_B + STATE_W
    C_DT = C_C + STATE_W
    C_GA = C_DT + NG * SH
    C_GB = C_GA + D
    FF = w_down.shape[1]
    KF = FF // P
    XT = (INNER + 2 * STATE_W) // P
    KI = INNER // P
    TAPS = ssd_conv_w.shape[1]
    NCP = (TAPS + 1) * XT
    FTAPS = ffn_conv_w.shape[1]
    PER_G = 7
    NR1 = KI + KD + 2 * KF + FTAPS * 2 * KF - P
    N_C1 = PER_G * NG
    N_C2 = N_C1 + 2 * NG
    N_D = N_C2 + 3 * NG
    N_E = N_D + KD // 2
    N_F = N_E + KF

    w_in, w_at, w_so = w_in[0], w_attn_out[0], w_ssd_out[0]
    w_o, w_u, w_d = w_out[0], w_up[0], w_down[0]
    x2, out2 = x[0], out[0]

    ctx = ExitStack()
    with ctx:
        def sb(name, shape, dt=F32, where=ctx):
            return where.enter_context(nc.sbuf_tensor(name, shape, dt))

        def sem(name):
            return ctx.enter_context(nc.semaphore(name))

        raw = [sb(f"raw{s}", [P, BLK]) for s in range(2)]
        whi = [sb(f"whi{s}", [P, BLK], F32R) for s in range(2)]
        wlo = [sb(f"wlo{s}", [P, BLK], F32R) for s in range(2)]
        uhi = sb("uhi", [P, KD, S], F32R)
        ulo = sb("ulo", [P, KD, S], F32R)
        oT = sb("oT", [P, KD, S])
        yT = sb("yT", [P, KI, S])
        ident = sb("ident", [P, P])
        par = sb("par", [P, 2, P])
        small = sb("small", [P, 64])
        fcw = sb("fcw", [P, FTAPS + 1, 2 * KF])
        fpar = sb("fpar", [P, 2, FTAPS + 1, 2])
        xin = yT[:, 0:8, :].rearrange("p a b -> p (a b)").rearrange("p (t d) -> p t d", t=NT)
        junk = yT[:, 8:16, :].rearrange("p a b -> p (a b)")

        gctx = ExitStack()
        prow = sb("prow", [P, 3, P], where=gctx)
        nrow = sb("nrow", [KD, P], where=gctx)
        posi = sb("posi", [NT, P], I32, where=gctx)
        hp = sb("hp", [P, 3, NG * SH], where=gctx)
        sinks = sb("sinks", [P, NG * QH], where=gctx)
        hpg = sb("hpg", [P, 3, SH], where=gctx)
        sinkg = sb("sinkg", [P, QH], where=gctx)
        cwg = sb("cwg", [P, TAPS + 1, 6], where=gctx)
        inv = sb("inv", [P, HALF], where=gctx)
        cosT = sb("cosT", [P, NT, HALF], where=gctx)
        sinT = sb("sinT", [P, NT, 2, HALF], where=gctx)
        tri = sb("tri", [P, P], where=gctx)
        above_f = sb("above_f", [P, P], where=gctx)
        ones = sb("ones", [P, P], where=gctx)
        above = sb("above", [P, P], F32R, where=gctx)
        qkv_sb = sb("qkv_sb", [P, NT, QKV], where=gctx)
        qk_rot = sb("qk_rot", [P, NT, QW + 2 * KW], where=gctx)
        rtmp = sb("rtmp", [P, QW + KW], where=gctx)
        va = sb("va", [P, NT + 1, HD], where=gctx)
        qT = sb("qT", [P, 2, S], where=gctx)
        kT = sb("kT", [P, S], where=gctx)
        conv = sb("conv", [P, 6, S], where=gctx)
        tanh_c = sb("tanh_c", [P, 2, S], where=gctx)
        b_tok = sb("b_tok", [P, S], where=gctx)
        x_tok = sb("x_tok", [P, NT, XW], where=gctx)
        seg_hi = sb("seg_hi", [P, 2, 512], F32R, where=gctx)
        seg_lo = sb("seg_lo", [P, 2, 512], F32R, where=gctx)
        decay_m = sb("decay_m", [P, SH, P], where=gctx)
        cb_m = sb("cb_m", [P, P], where=gctx)
        probs = sb("probs", [P, QH, P + 1], where=gctx)
        pT = sb("pT", [P, QH, P], where=gctx)
        tanh_z = sb("tanh_z", [P, XW], where=gctx)
        zg = sb("zg", [P, XW], where=gctx)
        xdt = sb("xdt", [P, XW], where=gctx)
        xdtd = sb("xdtd", [P, XW], where=gctx)
        xd = sb("xd", [P, XW], where=gctx)
        yv = sb("yv", [P, XW], where=gctx)
        state = sb("state", [P, XW], where=gctx)
        dtw = sb("dtw", [P, 6, NT * SH], where=gctx)
        dt_s = sb("dt_s", [P, NT, SH], where=gctx)
        adt = sb("adt", [P, NT * SH], where=gctx)
        adt_hi = sb("adt_hi", [P, NT * SH], F32R, where=gctx)
        adt_lo = sb("adt_lo", [P, NT * SH], F32R, where=gctx)
        dec = sb("dec", [P, 3, NT, SH], where=gctx)
        sm = sb("sm", [P, 4, QH], where=gctx)
        gctx.close()

        def two(v):
            return v.rearrange("p a b -> p (a b)")

        rhi = sb("rhi", [P, KF, S], F32R)
        rlo = sb("rlo", [P, KF, S], F32R)
        gt = sb("gt", [P, 2, S])
        tga = [gt[:, m, :] for m in range(2)]
        resid = xin
        work = yT[:, 8:16, :]
        squares = [two(oT[:, 4 + 2 * j:6 + 2 * j, :]) for j in range(2)]
        ahead_hi = [two(rhi[:, KF - 8 + 4 * q:KF - 4 + 4 * q, :]) for q in range(2)]
        ahead_lo = [two(rlo[:, KF - 8 + 4 * q:KF - 4 + 4 * q, :]) for q in range(2)]
        normw = oT[:, 0:4, :].rearrange("p a b -> p (a b)").rearrange("p (w d) -> p w d", w=2)

        ps = ctx.enter_context(nc.psum_tensor("ps", [P, 8, 512], F32))

        S_ = {}
        for name in (
            "x_in0", "x_in1", "x_in2", "x_in3", "consts_in", "par_in", "par2_in", "posT_ok", "pool_c", "loaded0", "loaded1", "hi_done", "lo_done", "blk_done",
            "dve_chain", "pool_chain", "xsq", "rstd", "xn", "xT_mm", "u_plain", "uhi_ok", "u_ok", "u2_ok", "parT_mm", "par_ok",
            "ang_ok", "rope_tab", "params_ok", "hp_ok",
            "qkv_mm", "qkv_sb", "roped", "va_ok", "dtabs", "dtexp", "dt_ok", "decay_mm", "decay_ok",
            "qkT_mm", "qkT_sb", "conv_mm", "tapped", "conv_ok", "tanhed", "silu_ok", "tok_mm", "tok_sb",
            "seg_hi_ok", "seg_lo_ok", "seg_mm", "lexp", "cb_mm", "cbm_ok", "s_mm", "smx", "sexp", "p_ok", "z_mm", "ztanh", "zg_ok",
            "m_ok", "pT_mm", "pT_sb", "y_mm", "y_done", "xdt_ok", "xdtd_ok", "xd_ok", "st_mm", "st_ok", "w_ok", "wsq",
            "yrstd", "yn_ok", "yT_mm", "yT_sb", "o_mm", "o_sb",
            "split_hi", "split_lo", "ga_mm", "ga_tanh", "at_mm", "at_ok", "gb_mm", "gb_tanh", "so_mm", "so_ok",
            "mg_hi", "mg_lo", "mg_lo2", "res_in", "out_mm", "d_sq", "d_rstd", "d_h", "h_sq", "h_rstd", "hn_ok", "hT_mm", "h_plain", "h_hi", "h_ok",
            "up_mm", "ftap", "fconv", "ftanh", "f_ok", "fhi_ok", "flo_ok", "fpar_ok", "dn_mm", "e_sq", "e_rstd", "e_ok", "stored",
        ):
            S_[name] = sem(name)
        s = S_
        loaded = [s["loaded0"], s["loaded1"]]
        x_in = [s[f"x_in{t}"] for t in range(NT)]

        block = ctx.enter_context(nc.Block())

        def bank(b, n=512):
            return ps[:, b, 0:n]

        def plain(t):
            return two(work[:, 2 * t:2 * t + 2, :]).rearrange("p (k c) -> p k c", k=KD)

        def tile_done(eng, G, f):
            if f % 2 == 0:
                eng.wait_ge(s["conv_mm"], G * 3 + (f // 2 + 1))
            else:
                eng.wait_ge(s["blk_done"], G * PER_G + (3 + f // 2))

        TOK_BANK = (0, 1, 1, 7, 6)

        def loaded_by(i, q, per=PER_G):
            return 64 * (i * per + q // 2 + 1)

        @block.sync
        def _(sp):
            def put(n, pieces):
                if n >= 2:
                    sp.wait_ge(s["lo_done"], n - 1)
                for dst, src in pieces:
                    sp.dma_start(dst, src).then_inc(loaded[n % 2], 64 // len(pieces))

            def rows_of(w, k0, nk, c0, width):
                return w[k0 * P:(k0 + nk) * P, c0:c0 + width].rearrange("(k p) n -> p k n", p=P)

            for t in range(2):
                sp.dma_start(xin[:, t, :], x2[t * P:(t + 1) * P, :]).then_inc(x_in[t], 16)
            sp.dma_start(nrow[:, :], mix_pre_norm[0].rearrange("(t c) -> t c", c=P)).then_inc(s["par_in"], 16)
            sp.dma_start(posi[:, :], positions[0].rearrange("(t c) -> t c", c=P)).then_inc(s["par_in"], 16)
            for t in range(2, NT):
                sp.dma_start(xin[:, t, :], x2[t * P:(t + 1) * P, :]).then_inc(x_in[t], 16)

            def late_parameters():
                for k in range(TAPS):
                    sp.dma_start(prow[k * XT:(k + 1) * XT, 0, :], ssd_conv_w[0, k].rearrange("(t c) -> t c", c=P)).then_inc(s["par2_in"], 16)
                sp.dma_start(prow[TAPS * XT:NCP, 0, :], ssd_conv_b[0].rearrange("(t c) -> t c", c=P)).then_inc(s["par2_in"], 16)
                rows = ffn_conv_w[0].rearrange("k (t c) -> (k t) c", c=P)
                sp.dma_start(prow[:, 2, :], rows[0:P]).then_inc(s["par2_in"], 16)
                at = 0
                for v in (ssd_norm[0], ffn_pre_norm[0], ffn_conv_b[0]):
                    n = v.shape[0] // P
                    sp.dma_start(prow[at:at + n, 1, :], v.rearrange("(t c) -> t c", c=P)).then_inc(s["par2_in"], 16)
                    at += n
                sp.dma_start(prow[at:at + FTAPS * 2 * KF - P, 1, :], rows[P:]).then_inc(s["par2_in"], 16)

            for g in range(NG):
                n = PER_G * g
                for h in range(2):
                    v = raw[(n + h) % 2][:, 0:4 * QKV].rearrange("p (k n) -> p k n", k=4)
                    put(n + h, [(v[:, :, 0:QW], rows_of(w_in, 4 * h, 4, g * QW, QW)),
                                (v[:, :, QW:QW + KW], rows_of(w_in, 4 * h, 4, C_K + g * KW, KW)),
                                (v[:, :, QW + KW:QW + 2 * KW], rows_of(w_in, 4 * h, 4, C_V + g * KW, KW)),
                                (v[:, :, QW + 2 * KW:QKV], rows_of(w_in, 4 * h, 4, C_DT + g * SH, SH))])
                    if g == 0 and h == 0:
                        late_parameters()
                if g == 0:
                    for j, v in enumerate((ssd_dt_bias, ssd_a_log, ssd_d)):
                        sp.dma_start(hp[:, j, :], v[0].partition_broadcast(P)).then_inc(s["consts_in"], 16)
                    sp.dma_start(sinks[:, :], attn_sinks[0].partition_broadcast(P)).then_inc(s["consts_in"], 16)
                v = raw[(n + 2) % 2].rearrange("p (k n) -> p k n", k=KD)
                put(n + 2, [(v[:, :, 0:P], rows_of(w_in, 0, KD, C_B + g * P, P)),
                            (v[:, :, P:2 * P], rows_of(w_in, 0, KD, C_C + g * P, P))])
                for r in range(2):
                    v = raw[(n + 3 + r) % 2].rearrange("p (k n) -> p k n", k=KD)
                    put(n + 3 + r, [(v, rows_of(w_in, 0, KD, C_X + g * XW + 256 * r, 256))])
                for h in range(2):
                    v = raw[(n + 5 + h) % 2].rearrange("p (k n) -> p k n", k=4)
                    put(n + 5 + h, [(v, rows_of(w_in, 4 * h, 4, C_Z + g * XW, XW))])

            def wide(sl):
                return raw[sl].rearrange("p (k n) -> p k n", k=KD)

            for i in range(NG):
                put(N_C1 + 2 * i, [(wide(0), rows_of(w_in, 0, KD, C_GA + 256 * i, 256))])
                put(N_C1 + 2 * i + 1, [(wide(1), rows_of(w_at, 0, KD, 256 * i, 256))])
            for i in range(NG):
                n = N_C2 + 3 * i
                put(n, [(wide(n % 2), rows_of(w_in, 0, KD, C_GB + 256 * i, 256))])
                for h in range(2):
                    put(n + 1 + h, [(wide((n + 1 + h) % 2), rows_of(w_so, h * KD, KD, 256 * i, 256))])
            for b in range(KD // 2):
                put(N_D + b, [(raw[b % 2].rearrange("p (k n) -> p k n", k=2), rows_of(w_o, 2 * b, 2, 0, D))])
                if b == 0:
                    sp.wait_ge(s["split_lo"], KD + KI)
                    sp.dma_start(resid, x2.rearrange("(t p) d -> p t d", p=P)).then_inc(s["res_in"], 16)
                if b == KD // 2 - 1:
                    sp.wait_ge(s["mg_lo"], KD - 2)
                    sp.dma_start(normw[:, 0, :], mix_post_norm[0].partition_broadcast(P)).then_inc(s["res_in"], 16)
                    sp.dma_start(normw[:, 1, :], ffn_post_norm[0].partition_broadcast(P)).then_inc(s["res_in"], 16)
            for j in range(KF):
                put(N_E + j, [(wide(j % 2)[:, :, h * P:(h + 1) * P], rows_of(w_u, 0, KD, FF * h + P * j, P)) for h in range(2)])
            for b in range(KF // 2):
                put(N_F + b, [(raw[b % 2].rearrange("p (k n) -> p k n", k=2), rows_of(w_d, 2 * b, 2, 0, D))])
            for t in range(NT - 1):
                sp.wait_ge(s["e_ok"], t + 1)
                sp.dma_start(out2[t * P:(t + 1) * P, :], two(work[:, 2 * t:2 * t + 2, :])).then_inc(s["stored"], 16)
            for h in range(2):
                sp.wait_ge(s["e_ok"], NT + h)
                sp.dma_start(out2[S - P:S, 512 * h:512 * h + 512], work[:, 2 * NT - 2 + h, :]).then_inc(s["stored"], 16)
            sp.wait_ge(s["stored"], 16 * (NT + 1))

        @block.gpsimd
        def _(pool):
            chain = [0]

            def link(ins):
                chain[0] += 1
                ins.then_inc(s["pool_chain"], 1)
                pool.wait_ge(s["pool_chain"], chain[0])

            for t_, v in ((ident, 0.0), (tri, 1.0), (above_f, 1.0)):
                link(pool.memset(t_[:, :], v))
            link(pool.memset(small[:, 0:1], -0.5))
            link(pool.memset(ones[:, :], 1.0))
            for k in range(HALF):
                f = float(bass_f32_inverse(k, HD))
                pool.memset(inv[:, k:k + 1], f).then_inc(s["pool_c"], 1)
            pool.affine_select(out=ident[:, :], in_=ident[:, :], compare_op=ALU.not_equal, fill=1.0, base=0,
                               pattern=[[-1, P]], channel_multiplier=1).then_inc(s["pool_c"], 1)
            pool.affine_select(out=tri[:, :], in_=tri[:, :], compare_op=ALU.is_ge, fill=0.0, base=0,
                               pattern=[[1, P]], channel_multiplier=-1).then_inc(s["pool_c"], 1)
            pool.affine_select(out=above_f[:, :], in_=above_f[:, :], compare_op=ALU.is_gt, fill=0.0, base=0,
                               pattern=[[-1, P]], channel_multiplier=1).then_inc(s["pool_c"], 1)

            def inverse_root(dst, ssum, scale, done):
                pool.tensor_scalar(dst, ssum, scale, EPS, ALU.mult, ALU.add).then_inc(s["pool_c"], 1)
                count[0] += 1
                pool.wait_ge(s["pool_c"], count[0])
                pool.tensor_tensor(dst, dst, small[:, 0:1], ALU.pow).then_inc(s[done], 1)

            count = [HALF + 3]
            def root_x(t):
                pool.wait_ge(s["xsq"], t + 1)
                inverse_root(small[:, 8 + t:9 + t], small[:, 4 + t:5 + t], 1.0 / D, "rstd")

            for t in range(NT):
                root_x(t)
            w0, w1 = tanh_c[:, 0, :], tanh_c[:, 1, :]
            NA = NT * HALF
            r3 = lambda a: a.rearrange("p (t k) -> p t k", t=NT)
            pool.wait_ge(s["posT_ok"], 1)
            link(pool.tensor_tensor(r3(w0[:, 0:NA]), small[:, 12:16].unsqueeze(2).to_broadcast([P, NT, HALF]),
                                    inv[:, :].unsqueeze(1).to_broadcast([P, NT, HALF]), ALU.mult))
            link(pool.tensor_scalar(w1[:, 0:NA], w0[:, 0:NA], 1.0 / 6.283185307179586, MAGIC, ALU.mult, ALU.add))
            link(pool.tensor_scalar(w1[:, 0:NA], w1[:, 0:NA], -MAGIC, None, ALU.add))
            for c in TWO_PI:
                link(pool.tensor_scalar(w1[:, NA:2 * NA], w1[:, 0:NA], -c, None, ALU.mult))
                link(pool.tensor_tensor(w0[:, 0:NA], w0[:, 0:NA], w1[:, NA:2 * NA], ALU.add))
            link(pool.tensor_scalar(w0[:, 0:NA], w0[:, 0:NA], PI, -PI, ALU.min, ALU.max))
            link(pool.tensor_scalar(w1[:, 0:NA], w0[:, 0:NA], 0.0, None, ALU.min))
            link(pool.tensor_scalar(w1[:, NA:2 * NA], w0[:, 0:NA], 0.0, None, ALU.max))
            link(pool.tensor_tensor(w1[:, NA:2 * NA], w1[:, NA:2 * NA], w1[:, 0:NA], ALU.subtract))
            pool.tensor_scalar(w0[:, NA:2 * NA], w1[:, NA:2 * NA], -1.0, 1.5707963267948966, ALU.mult, ALU.add).then_inc(s["ang_ok"], 1)
            for t in range(NT):
                pool.wait_ge(s["uhi_ok"], t + 1)
                c = slice(t * P, (t + 1) * P)
                pool.tensor_tensor(ulo[:, KD // 2:, c], plain(t)[:, KD // 2:, :], uhi[:, KD // 2:, c].bitcast(F32),
                                   ALU.subtract).then_inc(s["u2_ok"], 1)
            base = count[0]

            def group(i, p):
                G = i * 2 + p
                def build(t):
                    for q in range(2):
                        a = adt_lo[:, t * SH + 4 * q:t * SH + 4 * q + 4].bitcast(F32)
                        pool.tensor_tensor(seg_lo[:, q, :].rearrange("p (h l) -> p h l", h=4),
                                           tri[:, :].unsqueeze(1).to_broadcast([P, 4, P]),
                                           a.unsqueeze(2).to_broadcast([P, 4, P]), ALU.mult).then_inc(s["seg_lo_ok"], 1)

                pool.wait_ge(s["dt_ok"], G + 1)
                pool.wait_ge(s["seg_mm"], G * 2 * NT)
                build(0)
                view = lambda b: b[:, :].rearrange("p (h d) -> p h d", h=SH)
                bc = lambda a: a.unsqueeze(2).to_broadcast([P, SH, HD])
                for t in range(NT):
                    T = G * NT + t
                    if t < NT - 1:
                        pool.wait_ge(s["seg_mm"], T * 2 + 2)
                        build(t + 1)
                    if t == 0:
                        pool.wait_ge(s["decay_ok"], G + 1)
                        pool.wait_ge(s["y_mm"], T)
                    else:
                        pool.wait_ge(s["st_mm"], G * (NT - 1) + t)
                    pool.wait_ge(s["xdt_ok"], T + 1)
                    pool.tensor_tensor(view(xdtd), view(xdt), bc(dec[:, 0, t, :]), ALU.mult).then_inc(s["xdtd_ok"], 1)
                    pool.wait_ge(s["w_ok"], T)
                    pool.tensor_tensor(view(xd), x_tok[:, t, :].rearrange("p (h d) -> p h d", h=SH), bc(hpg[:, 2, :]),
                                       ALU.mult).then_inc(s["xd_ok"], 1)
                    pool.wait_ge(s["pool_c"], HALF + 3)
                    pool.wait_ge(s["wsq"], T + 1)
                    pool.tensor_scalar(small[:, 20:21], small[:, 16:17], 1.0 / (4 * XW), EPS, ALU.mult,
                                       ALU.add).then_inc(s["pool_c"], 1)
                    pool.wait_ge(s["pool_c"], T + (base + 1))
                    pool.wait_ge(s["yn_ok"], T)
                    pool.tensor_tensor(small[:, 17:18], small[:, 20:21], small[:, 0:1], ALU.pow).then_inc(s["yrstd"], 1)

            with pool.Fori(0, NG // 2) as i:
                group(i, 0)
                group(i, 1)
            count[0] = base + NG * NT
            for k in range(KD - 2):
                pool.wait_ge(s["mg_hi"], k + 1)
                pool.tensor_tensor(ulo[:, k, :], oT[:, k, :], uhi[:, k, :].bitcast(F32), ALU.subtract).then_inc(s["mg_lo"], 1)
            for name, t in (("d", 0), ("d", 1), ("h", 0), ("h", 1), ("d", 2), ("d", 3), ("h", 2), ("h", 3)):
                if name == "d":
                    pool.wait_ge(s["d_sq"], t + 1)
                    inverse_root(small[:, 28 + t:29 + t], small[:, 24 + t:25 + t], 1.0 / D, "d_rstd")
                else:
                    pool.wait_ge(s["h_sq"], t + 1)
                    inverse_root(small[:, 36 + t:37 + t], small[:, 32 + t:33 + t], 1.0 / D, "h_rstd")
            for t in range(NT - 1):
                pool.wait_ge(s["e_sq"], t + 1)
                inverse_root(small[:, 48 + t:49 + t], small[:, 40 + t:41 + t], 1.0 / D, "e_rstd")
            c = 48 + NT - 1
            pool.wait_ge(s["e_sq"], NT)
            link(pool.tensor_scalar(small[:, c:c + 1], small[:, 39 + NT:40 + NT], 1.0 / D, EPS, ALU.mult, ALU.add))
            pool.wait_ge(s["e_sq"], NT + 1)
            link(pool.tensor_scalar(small[:, c:c + 1], small[:, 40 + NT:41 + NT], 1.0 / D, small[:, c:c + 1], ALU.mult, ALU.add))
            pool.tensor_tensor(small[:, c:c + 1], small[:, c:c + 1], small[:, 0:1], ALU.pow).then_inc(s["e_rstd"], 1)

        @block.scalar
        def _(act):
            def hi(sl, landed, n_next, width=BLK, into=None):
                act.wait_ge(loaded[sl], landed)
                if n_next is not None:
                    act.wait_ge(s["blk_done"], n_next)
                act.activation(whi[sl][:, 0:width] if into is None else into, raw[sl][:, 0:width], ACT.Copy).then_inc(s["hi_done"], 1)

            def square_x(t):
                act.wait_ge(x_in[t], 16)
                act.activation(junk[:, t * D:(t + 1) * D], xin[:, t, :], ACT.Square,
                               accum_out=small[:, 4 + t:5 + t]).then_inc(s["xsq"], 1)

            def u_hi(t):
                act.wait_ge(s["par_ok"], 1)
                act.wait_ge(s["u_plain"], t + 1)
                act.activation(uhi[:, :, t * P:(t + 1) * P], plain(t), ACT.Copy).then_inc(s["uhi_ok"], 1)

            square_x(0)
            square_x(1)
            act.wait_ge(s["parT_mm"], 2)
            act.activation(par[:, 0, NCP:NCP + KD], ps[:, 7, 0:KD], ACT.Copy).then_inc(s["par_ok"], 1)
            act.activation(small[:, 12:16], ps[:, 7, KD:KD + NT], ACT.Copy).then_inc(s["posT_ok"], 1)
            square_x(2)
            square_x(3)
            u_hi(0)
            hi(0, 64, None, 4 * QKV)
            u_hi(1)
            act.wait_ge(s["parT_mm"], 5)
            act.activation(par[:, 0, 0:NCP], ps[:, 3, NR1 + P:NR1 + P + NCP], ACT.Copy, scale=0.5).then_inc(s["par_ok"], 1)
            act.activation(par[:, 1, 0:KI], ps[:, 3, 0:KI], ACT.Copy, scale=0.5).then_inc(s["par_ok"], 1)
            act.activation(par[:, 1, KI:NR1], ps[:, 3, KI:NR1], ACT.Copy).then_inc(s["par_ok"], 1)
            act.activation(fcw[:, :, :].rearrange("p k t -> p (k t)")[:, 0:P], ps[:, 3, NR1:NR1 + P], ACT.Copy).then_inc(s["par_ok"], 1)
            u_hi(2)
            hi(1, 64, None, 4 * QKV)
            u_hi(3)
            act.wait_ge(s["ang_ok"], 1)
            act.activation(sinT[:, :, 1, :], tanh_c[:, 0, 0:NT * HALF].rearrange("p (t k) -> p t k", t=NT), ACT.Sin).then_inc(s["rope_tab"], 1)
            act.activation(cosT[:, :, :], tanh_c[:, 0, NT * HALF:2 * NT * HALF].rearrange("p (t k) -> p t k", t=NT), ACT.Sin).then_inc(s["rope_tab"], 1)
            act.wait_ge(s["consts_in"], 64)
            act.activation(hp[:, 1, :], hp[:, 1, :], ACT.Exp).then_inc(s["hp_ok"], 1)

            def group(i, p):
                G = i * 2 + p

                def hi_next(j, width=BLK):
                    q = PER_G * p + j + 1
                    hi(q % 2, loaded_by(i, q), G * PER_G + j, width)

                def tap(f):
                    tile_done(act, G, f)
                    act.activation(conv[:, f, :], bank(4 + f % 4), ACT.Identity, scale=cwg[:, TAPS - 1, f:f + 1],
                                   bias=cwg[:, TAPS, f:f + 1]).then_inc(s["tapped"], 1)

                def tanh(f):
                    act.wait_ge(s["conv_ok"], G * 6 + (f + 1))
                    act.activation(tanh_c[:, f % 2, :], conv[:, f, :], ACT.Tanh).then_inc(s["tanhed"], 1)

                def turn_y(t, first_tile, b):
                    act.activation(yT[:, bass.ds(first_tile, 4), t * P:(t + 1) * P],
                                   bank(b).rearrange("p (f c) -> p f c", f=4), ACT.Copy).then_inc(s["yT_sb"], 1)

                def tok(f):
                    act.wait_ge(s["tok_mm"], G * 5 + (f + 1))
                    if f == 0:
                        act.activation(b_tok[:, :], bank(0), ACT.Copy).then_inc(s["tok_sb"], 1)
                    else:
                        act.activation(x_tok[:, :, (f - 1) * P:f * P], bank(TOK_BANK[f]).rearrange("p (t c) -> p t c", t=NT),
                                       ACT.Copy).then_inc(s["tok_sb"], 1)

                def build(t):
                    for h in range(SH):
                        act.activation(seg_hi[:, h // 4, (h % 4) * P:(h % 4 + 1) * P], tri[:, :], ACT.Copy,
                                       scale=adt_hi[:, t * SH + h:t * SH + h + 1].bitcast(F32)).then_inc(s["seg_hi_ok"], 1)

                act.wait_ge(s["u2_ok"], NT)
                act.wait_ge(s["yT_mm"], G * NT + 1)
                turn_y(NT - 1, i * 8 if p else i * (-8) + 12, 7)
                hi_next(1)
                for t in range(NT):
                    if t < NT - 1:
                        act.wait_ge(s["qkv_mm"], G * (NT - 1) + (t + 1))
                    else:
                        act.wait_ge(s["blk_done"], G * PER_G + 2)
                    if t == 0:
                        act.wait_ge(s["o_mm"], G * NT)
                    vc = slice(QW + KW, QW + 2 * KW)
                    act.activation(va[0:64, t, :], ps[0:64, t, vc], ACT.Copy).then_inc(s["va_ok"], 1)
                    act.activation(va[64:128, t + 1, :], ps[64:128, t, vc], ACT.Copy).then_inc(s["va_ok"], 1)
                    act.activation(qkv_sb[:, t, :], bank(t, QKV), ACT.Copy).then_inc(s["qkv_sb"], 1)
                hi_next(2)
                act.wait_ge(s["params_ok"], G * 5 + 5)
                act.wait_ge(s["y_mm"], G * NT)
                tap(0)
                act.wait_ge(s["dtabs"], G + 1)
                act.activation(dtw[:, 2, :], dtw[:, 1, :], ACT.Exp, scale=-1.0).then_inc(s["dtexp"], 1)
                tap(1)
                tanh(0)
                hi_next(3)
                tap(2)
                tanh(1)
                tap(3)
                act.wait_ge(s["dt_ok"], G + 1)
                act.wait_ge(s["seg_mm"], G * 2 * NT)
                build(0)
                tanh(2)
                hi_next(4)
                tap(4)
                tanh(3)
                tap(5)
                for j in range(3):
                    act.wait_ge(s["qkT_mm"], G * 3 + (j + 1))
                    act.activation(qT[:, j, :] if j < 2 else kT[:, :], bank(j), ACT.Copy,
                                   scale=HD ** -0.5 if j < 2 else 1.0).then_inc(s["qkT_sb"], 1)
                act.wait_ge(s["decay_mm"], G + 1)
                act.activation(dec[:, :, :, :].rearrange("p a t h -> p (a t h)"), bank(3, 3 * NT * SH), ACT.Exp).then_inc(s["decay_ok"], 1)
                tok(0)
                tanh(4)
                tanh(5)

                for t in range(NT):
                    T = G * NT + t
                    for q in range(2):
                        act.wait_ge(s["seg_mm"], T * 2 + (q + 1))
                        act.wait_ge(s["y_mm"], T)
                        act.activation(decay_m[:, 4 * q:4 * q + 4, :].rearrange("p h l -> p (h l)"), bank(2 + q),
                                       ACT.Exp).then_inc(s["lexp"], 1)

                    def softmax_exp():
                        act.wait_ge(s["smx"], T + 1)
                        pr = probs[:, :, :].rearrange("p h l -> p (h l)")
                        act.activation(pr, pr, ACT.Exp).then_inc(s["sexp"], 1)

                    if t == 0:
                        hi_next(5)
                        act.wait_ge(s["xd_ok"], G * NT)
                        tok(1)
                        tok(2)
                        tok(3)
                        tok(4)
                        act.wait_ge(s["seg_mm"], T * 2 + 2)
                        build(1)
                    softmax_exp()
                    if t == NT - 1:
                        hi_next(6, BLK if p else 4 * QKV)
                    elif t:
                        act.wait_ge(s["seg_mm"], T * 2 + 2)
                        build(t + 1)
                    if t < NT - 1:
                        act.wait_ge(s["z_mm"], G * (NT - 1) + (t + 1))
                    else:
                        act.wait_ge(s["blk_done"], G * PER_G + PER_G)
                    act.wait_ge(s["zg_ok"], T)
                    act.wait_ge(s["wsq"], T)
                    act.activation(tanh_z[:, :], bank(t % 2), ACT.Tanh, scale=0.5).then_inc(s["ztanh"], 1)
                    if t:
                        act.wait_ge(s["yT_mm"], G * NT + (t + 1))
                        turn_y(t - 1, G * 4, 3)
                    act.wait_ge(s["pT_mm"], T + 1)
                    act.activation(pT[:, :, :].rearrange("p h l -> p (h l)"), bank(4), ACT.Copy).then_inc(s["pT_sb"], 1)
                    act.wait_ge(s["o_mm"], T + 1)
                    act.activation(oT[:, bass.ds(G * 2, 2), t * P:(t + 1) * P],
                                   bank(4, 2 * P).rearrange("p (f c) -> p f c", f=2), ACT.Copy, scale=0.5).then_inc(s["o_sb"], 1)
                    act.wait_ge(s["w_ok"], T + 1)
                    act.activation(tanh_z[:, :], yv[:, :], ACT.Square, accum_out=small[:, 16:17]).then_inc(s["wsq"], 1)
                hi_next(7, BLK if p else 4 * QKV)

            with act.Fori(0, NG // 2) as i:
                group(i, 0)
                group(i, 1)

            act.wait_ge(s["o_sb"], NG * NT)
            for k in range(KD):
                act.activation(rhi[:, KD + k, :], oT[:, k, :], ACT.Copy).then_inc(s["split_hi"], 1)
            act.wait_ge(s["yT_mm"], NG * NT + 1)
            act.activation(yT[:, KI - 4:KI, (NT - 1) * P:S], bank(7).rearrange("p (f c) -> p f c", f=4), ACT.Copy).then_inc(s["yT_sb"], 1)
            SN = 0
            for k in range(KD):
                act.activation(rhi[:, k, :], yT[:, k, :], ACT.Copy, scale=par[:, 1, SN + k:SN + k + 1]).then_inc(s["split_hi"], 1)

            def gate_a(i, first=False):
                n = i * 2 + N_C1
                if not first:
                    hi(1, 64 * (i + (N_C1 // 2 + 1)), n)
                for m in range(2):
                    if m == 0:
                        act.wait_ge(s["ga_mm"], i + 1)
                    else:
                        act.wait_ge(s["blk_done"], n + 1)
                    act.wait_ge(s["at_ok"], i * 2)
                    act.activation(tga[m], bank(m), ACT.Tanh, scale=0.5).then_inc(s["ga_tanh"], 1)
                hi(0, 64 * (i + (N_C1 // 2 + 2)), n + 1)

            gate_a(0, True)
            with act.Fori(1, NG) as i:
                gate_a(i)
            act.wait_ge(s["at_ok"], 2 * NG)
            act.wait_ge(s["blk_done"], N_C2)
            for k in range(KD, KI):
                act.activation(rhi[:, k, :], yT[:, k, :], ACT.Copy, scale=par[:, 1, SN + k:SN + k + 1]).then_inc(s["split_hi"], 1)
            with act.Fori(0, NG // 2) as i:
                for q in range(6):
                    r, j = divmod(q, 3)
                    n = i * 6 + (N_C2 + q)
                    hi((q + 1) % 2, 64 * (i * 3 + ((N_C2 + q + 1) // 2 + 1)), n)
                    if j == 0:
                        for m in range(2):
                            if m == 0:
                                act.wait_ge(s["gb_mm"], i * 2 + (r + 1))
                            else:
                                act.wait_ge(s["blk_done"], n + 1)
                            act.wait_ge(s["so_ok"], i * 4 + 2 * r)
                            act.activation(tga[m], bank(4 + m), ACT.Tanh, scale=0.5).then_inc(s["gb_tanh"], 1)
            act.wait_ge(s["blk_done"], N_D - 2)
            for k in range(KD):
                act.wait_ge(s["so_ok"], k + 1)
                act.activation(uhi[:, k, :], oT[:, k, :], ACT.Copy).then_inc(s["mg_hi"], 1)
            def hi_of(n):
                hi(n % 2, 64 * (n // 2 + 1), n - 1)

            def h_hi(t):
                act.wait_ge(s["h_plain"], t + 1)
                act.activation(uhi[:, :, t * P:(t + 1) * P], plain(t), ACT.Copy).then_inc(s["h_hi"], 1)

            def out_square(t):
                if t < NT - 1:
                    act.wait_ge(s["out_mm"], t + 1)
                else:
                    act.wait_ge(s["blk_done"], N_E)
                if t:
                    act.wait_ge(s["d_sq"], t)
                act.activation(squares[0], two(ps[:, 2 * t:2 * t + 2, :]), ACT.Square,
                               accum_out=small[:, 24 + t:25 + t]).then_inc(s["d_sq"], 1)

            def h_square(t):
                act.wait_ge(s["d_h"], t + 1)
                if t:
                    act.wait_ge(s["h_sq"], t)
                act.activation(squares[1], resid[:, t, :], ACT.Square,
                               accum_out=small[:, 32 + t:33 + t]).then_inc(s["h_sq"], 1)

            def h_norm(t):
                act.wait_ge(s["h_rstd"], t + 1)
                act.activation(two(work[:, 2 * t:2 * t + 2, :]), resid[:, t, :], ACT.Copy,
                               scale=small[:, 36 + t:37 + t]).then_inc(s["hn_ok"], 1)

            for b in range(1, KD // 2):
                hi_of(N_D + b)
            hi(0, 64 * (N_E // 2 + 1), N_D, into=ahead_hi[0])
            out_square(0)
            hi(1, 64 * (N_E // 2 + 1), N_D, into=ahead_hi[1])
            out_square(1)
            h_square(0)
            h_norm(0)
            h_square(1)
            out_square(2)
            h_norm(1)
            h_hi(0)
            h_hi(1)
            out_square(3)
            h_square(2)
            h_norm(2)
            h_square(3)
            h_norm(3)
            h_hi(2)
            h_hi(3)
            for q in range(2):
                hi(q, 64 * (N_E // 2 + 2), N_E - 1 + q)

            def up(i, first=False):
                for q in range(2):
                    n = i * 2 + (N_E + q)
                    J = i * 2 + q
                    act.wait_ge(s["fpar_ok"], J * 2 + 2)
                    act.wait_ge(s["f_ok"], J)
                    for v in range(2):
                        if v == 0:
                            act.wait_ge(s["up_mm"], J + 1)
                        else:
                            act.wait_ge(s["blk_done"], n + 1)
                        act.activation(work[:, v, :], bank(2 * q + v), ACT.Identity, scale=fpar[:, q, FTAPS - 1, v:v + 1],
                                       bias=fpar[:, q, FTAPS, v:v + 1]).then_inc(s["ftap"], 1)
                    if not first:
                        hi(q, 64 * (i + ((N_E + q + 2) // 2 + 1)), n + 1)
                    act.wait_ge(s["fconv"], J + 1)
                    act.activation(work[:, 2, :], work[:, 0, :], ACT.Tanh).then_inc(s["ftanh"], 1)
                    act.wait_ge(s["f_ok"], J + 1)
                    act.activation(rhi[:, bass.ds(J, 1), :], work[:, 3:4, :], ACT.Copy).then_inc(s["fhi_ok"], 1)

            up(0, True)
            with act.Fori(1, KF // 2) as i:
                up(i)
            for b in range(2, KF // 2):
                hi_of(N_F + b)
            for t in range(NT - 1):
                act.wait_ge(s["dn_mm"], t + 1)
                if t:
                    act.wait_ge(s["e_sq"], t)
                act.activation(squares[0], two(ps[:, 2 * t:2 * t + 2, :]), ACT.Square,
                               accum_out=small[:, 40 + t:41 + t]).then_inc(s["e_sq"], 1)
            for h in range(2):
                if h == 0:
                    act.wait_ge(s["dn_mm"], NT)
                else:
                    act.wait_ge(s["blk_done"], N_F + KF // 2)
                act.activation(squares[1][:, 512 * h:512 * h + 512], bank(2 * NT - 2 + h), ACT.Square,
                               accum_out=small[:, 39 + NT + h:40 + NT + h]).then_inc(s["e_sq"], 1)

        @block.vector
        def _(dve):
            links = {"n": 0, "base": 0}

            def link(ins):
                links["n"] += 1
                ins.then_inc(s["dve_chain"], 1)
                dve.wait_ge(s["dve_chain"], links["base"] + links["n"])

            def lo(sl, done, width=BLK, h=None, into=None):
                dve.wait_ge(s["hi_done"], done)
                h = whi[sl][:, 0:width] if h is None else h
                dve.tensor_tensor(wlo[sl][:, 0:width] if into is None else into, raw[sl][:, 0:width], h.bitcast(F32),
                                  ALU.subtract).then_inc(s["lo_done"], 1)

            def heads(a, n, w):
                return a.unsqueeze(2).to_broadcast([P, n, w])

            dve.wait_ge(s["pool_c"], HALF + 3)
            link(dve.tensor_copy(above[:, :], above_f[:, :]))
            link(dve.memset(yv[:, :], 0.0))
            dve.wait_ge(s["par_in"], 16 * 2)
            link(dve.tensor_copy(rtmp[0:NT, 0:P], posi[:, :]))

            def weigh(t, turned, weight, done):
                dve.wait_ge(s[turned], t + 1)
                dve.tensor_tensor(plain(t), two(ps[:, 2 * t:2 * t + 2, :]).rearrange("p (k c) -> p k c", k=KD),
                                  weight.unsqueeze(2).to_broadcast([P, KD, P]), ALU.mult).then_inc(s[done], 1)

            def rest(t, hi_name, done, n=KD):
                dve.wait_ge(s[hi_name], t + 1)
                c = slice(t * P, (t + 1) * P)
                dve.tensor_tensor(ulo[:, 0:n, c], plain(t)[:, 0:n, :], uhi[:, 0:n, c].bitcast(F32), ALU.subtract).then_inc(s[done], 1)

            def scale_x(t):
                dve.wait_ge(s["rstd"], t + 1)
                dve.tensor_scalar(xin[:, t, :], xin[:, t, :], small[:, 8 + t:9 + t], None, ALU.mult).then_inc(s["xn"], 1)

            def weigh_x(t):
                dve.wait_ge(s["par_ok"], 1)
                weigh(t, "xT_mm", par[:, 0, NCP:NCP + KD], "u_plain")

            def rest_x(t):
                rest(t, "uhi_ok", "u_ok", KD // 2)

            scale_x(0)
            scale_x(1)
            weigh_x(0)
            scale_x(2)
            scale_x(3)
            weigh_x(1)
            rest_x(0)
            lo(0, 1, 4 * QKV)
            weigh_x(2)
            rest_x(1)
            weigh_x(3)
            rest_x(2)
            rest_x(3)
            lo(1, 2, 4 * QKV)
            dve.wait_ge(s["par_ok"], 5)
            fl = fcw[:, :, :].rearrange("p k t -> p (k t)")
            nb = KI + KD
            link(dve.tensor_copy(fl[:, P:FTAPS * 2 * KF], par[:, 1, nb + 2 * KF:nb + FTAPS * 2 * KF - P + 2 * KF]))
            link(dve.tensor_copy(fl[:, FTAPS * 2 * KF:], par[:, 1, nb:nb + 2 * KF]))
            link(dve.tensor_scalar(fcw[:, :, 0:KF], fcw[:, :, 0:KF], 0.5, None, ALU.mult))
            dve.wait_ge(s["rope_tab"], 2)
            link(dve.tensor_scalar(sinT[:, :, 0, :], sinT[:, :, 1, :], -1.0, None, ALU.mult))
            dve.wait_ge(s["hp_ok"], 1)
            link(dve.tensor_scalar(hp[:, 1, :], hp[:, 1, :], -1.0, None, ALU.mult))
            before = links["n"]

            def group(i, p):
                G = i * 2 + p
                Q0 = PER_G * p

                def lo_next(j, width=BLK):
                    lo((Q0 + j + 1) % 2, G * PER_G + (j + 2), width)

                def taps(f):
                    dve.wait_ge(s["tapped"], G * 6 + (f + 1))
                    for k in range(TAPS - 2, -1, -1):
                        sh = TAPS - 1 - k
                        ins = dve.scalar_tensor_tensor(out=conv[:, f, sh:], in0=ps[:, 4 + f % 4, 0:S - sh],
                                                       scalar=cwg[:, k, f:f + 1], in1=conv[:, f, sh:], op0=ALU.mult, op1=ALU.add)
                        if k:
                            link(ins)
                        else:
                            ins.then_inc(s["conv_ok"], 1)

                def silu(f):
                    dve.wait_ge(s["tanhed"], G * 6 + (f + 1))
                    dve.scalar_tensor_tensor(out=conv[:, f, :], in0=tanh_c[:, f % 2, :], scalar=1.0, in1=conv[:, f, :],
                                             op0=ALU.add, op1=ALU.mult).then_inc(s["silu_ok"], 1)

                dve.wait_ge(s["xd_ok"], G * NT)
                cw = par[:, 0, 0:NCP].rearrange("p (k t) -> p k t", k=TAPS + 1)
                dve.tensor_copy(cwg[:, :, 2:6], cw[:, :, bass.ds(G * 4, 4)]).then_inc(s["params_ok"], 1)
                dve.tensor_copy(cwg[:, :, 0:1], cw[:, :, bass.ds(G + INNER // P, 1)]).then_inc(s["params_ok"], 1)
                dve.tensor_copy(cwg[:, :, 1:2], cw[:, :, bass.ds(G + (INNER + STATE_W) // P, 1)]).then_inc(s["params_ok"], 1)
                dve.tensor_copy(hpg[:, :, :], hp[:, :, bass.ds(G * SH, SH)]).then_inc(s["params_ok"], 1)
                dve.tensor_copy(sinkg[:, :].rearrange("p (a b) -> p a b", a=2),
                                sinks[:, bass.ds(G * QH, QH)].rearrange("p (b a) -> p a b", a=2)).then_inc(s["params_ok"], 1)
                dve.wait_ge(s["params_ok"], G * 5 + 5)
                lo_next(1)
                for t in range(NT):
                    dve.wait_ge(s["qkv_sb"], G * NT + (t + 1))
                    if t == 0:
                        dve.wait_ge(s["qkT_mm"], G * 3)
                    src = qkv_sb[:, t, 0:QW + KW].rearrange("p (h r k) -> p h r k", r=2, k=HALF)
                    dst = qk_rot[:, t, 0:QW + KW].rearrange("p (h r k) -> p h r k", r=2, k=HALF)
                    tmp = rtmp[:, :].rearrange("p (h r k) -> p h r k", r=2, k=HALF)
                    cs = cosT[:, t, :].unsqueeze(1).unsqueeze(1).to_broadcast([P, QH + 1, 2, HALF])
                    link(dve.tensor_tensor(dst, src, cs, ALU.mult))
                    for r in range(2):
                        link(dve.tensor_tensor(tmp[:, :, r, :], src[:, :, 1 - r, :],
                                               sinT[:, t, r, :].unsqueeze(1).to_broadcast([P, QH + 1, HALF]), ALU.mult))
                    link(dve.tensor_tensor(qk_rot[:, t, 0:QW + KW], qk_rot[:, t, 0:QW + KW], rtmp[:, :], ALU.add))
                    dve.tensor_copy(qk_rot[:, t, QW + KW:], qk_rot[:, t, QW:QW + KW]).then_inc(s["roped"], 1)
                    if t == 1:
                        lo_next(2)
                b3 = lambda a: a.rearrange("p (t h) -> p t h", t=NT)
                link(dve.tensor_tensor(b3(dtw[:, 0, :]), qkv_sb[:, :, QW + 2 * KW:QKV],
                                       hpg[:, 0, :].unsqueeze(1).to_broadcast([P, NT, SH]), ALU.add))
                dve.scalar_tensor_tensor(out=dtw[:, 1, :], in0=dtw[:, 0, :], scalar=-1.0, in1=dtw[:, 0, :],
                                         op0=ALU.mult, op1=ALU.max).then_inc(s["dtabs"], 1)
                taps(0)
                dve.wait_ge(s["dtexp"], G + 1)
                link(dve.tensor_scalar(dtw[:, 3, :], dtw[:, 2, :], 2.0, None, ALU.add))
                link(dve.reciprocal(dtw[:, 3, :], dtw[:, 3, :]))
                link(dve.tensor_tensor(dtw[:, 4, :], dtw[:, 2, :], dtw[:, 3, :], ALU.mult))
                link(dve.tensor_tensor(dtw[:, 5, :], dtw[:, 4, :], dtw[:, 4, :], ALU.mult))
                link(dve.tensor_scalar(dtw[:, 3, :], dtw[:, 5, :], 1.0 / 17, None, ALU.mult))
                for d in range(15, 1, -2):
                    link(dve.scalar_tensor_tensor(out=dtw[:, 3, :], in0=dtw[:, 3, :], scalar=1.0 / d, in1=dtw[:, 5, :],
                                                  op0=ALU.add, op1=ALU.mult))
                link(dve.scalar_tensor_tensor(out=dtw[:, 3, :], in0=dtw[:, 3, :], scalar=1.0, in1=dtw[:, 4, :],
                                              op0=ALU.add, op1=ALU.mult))
                link(dve.tensor_scalar(dtw[:, 0, :], dtw[:, 0, :], 0.0, None, ALU.max))
                dts = dt_s[:, :, :].rearrange("p t h -> p (t h)")
                link(dve.scalar_tensor_tensor(out=dts, in0=dtw[:, 3, :], scalar=2.0, in1=dtw[:, 0, :], op0=ALU.mult, op1=ALU.add))
                link(dve.tensor_tensor(b3(adt[:, :]), dt_s[:, :, :], hpg[:, 1, :].unsqueeze(1).to_broadcast([P, NT, SH]), ALU.mult))
                link(dve.tensor_copy(adt_hi[:, :], adt[:, :]))
                dve.tensor_tensor(adt_lo[:, :], adt[:, :], adt_hi[:, :].bitcast(F32), ALU.subtract).then_inc(s["dt_ok"], 1)
                taps(1)
                silu(0)
                lo_next(3)
                taps(2)
                silu(1)
                taps(3)
                silu(2)
                lo_next(4)
                taps(4)
                silu(3)
                taps(5)
                silu(4)
                silu(5)

                h8 = lambda b: b.rearrange("p (h d) -> p h d", h=SH)

                def norm_y(T):
                    dve.wait_ge(s["yrstd"], T + 1)
                    dve.tensor_scalar(yv[:, :], yv[:, :], small[:, 17:18], 0.5, ALU.mult, ALU.mult).then_inc(s["yn_ok"], 1)

                for t in range(NT):
                    T = G * NT + t
                    dve.wait_ge(s["cb_mm"], T + 1)
                    dve.tensor_tensor(cb_m[:, :], bank(6, P), tri[:, :], ALU.mult).then_inc(s["cbm_ok"], 1)

                    def mask_decays(quads):
                        for q in quads:
                            dve.wait_ge(s["lexp"], T * 2 + (q + 1))
                            if q == 0:
                                dve.wait_ge(s["cbm_ok"], T + 1)
                            m = decay_m[:, 4 * q:4 * q + 4, :]
                            dve.tensor_tensor(m, m, cb_m[:, :].unsqueeze(1).to_broadcast([P, 4, P]), ALU.mult).then_inc(s["m_ok"], 1)

                    def times_dt():
                        dve.wait_ge(s["y_mm"], T)
                        if t == 0:
                            dve.wait_ge(s["tok_sb"], G * 5 + 5)
                        dve.tensor_tensor(h8(xdt[:, :]), h8(x_tok[:, t, :]), heads(dt_s[:, t, :], SH, HD), ALU.mult).then_inc(s["xdt_ok"], 1)

                    if t == 0:
                        mask_decays(range(2))
                        lo_next(5)
                    dve.wait_ge(s["s_mm"], T + 1)
                    sc = ps[:, 4:6, 0:2 * P].rearrange("p a (b k) -> p a b k", b=2)
                    pr = probs[:, :, :].rearrange("p (a b) k -> p a b k", a=2)
                    mx = sm[:, 1, :].rearrange("p (a b) -> p a b", a=2)
                    if t == 0:
                        link(dve.memset(sc[0:64, :, :, 64:P], MASKED))
                    link(dve.tensor_reduce(sm[:, 0, :].rearrange("p (a b) -> p a b", a=2), sc, AX_X, ALU.max))
                    link(dve.tensor_tensor(sm[:, 1, :], sm[:, 0, :], sinkg[:, :], ALU.max))
                    dve.wait_ge(s["pT_mm"], T)
                    link(dve.tensor_tensor(pr[:, :, :, 0:P], sc, mx.unsqueeze(3).to_broadcast([P, 2, 2, P]), ALU.subtract))
                    dve.tensor_tensor(probs[:, :, P:P + 1], sinkg[:, :].unsqueeze(2), sm[:, 1, :].unsqueeze(2),
                                      ALU.subtract).then_inc(s["smx"], 1)
                    if t:
                        norm_y(T - 1)
                    else:
                        times_dt()
                    if t:
                        mask_decays((0,))
                    dve.wait_ge(s["sexp"], T + 1)
                    link(dve.tensor_reduce(sm[:, 2, :], probs[:, :, :], AX_X, ALU.add))
                    link(dve.reciprocal(sm[:, 3, :], sm[:, 2, :]))
                    dve.tensor_tensor(probs[:, :, 0:P], probs[:, :, 0:P], heads(sm[:, 3, :], QH, P), ALU.mult).then_inc(s["p_ok"], 1)
                    if t:
                        mask_decays((1,))
                        times_dt()
                    if t == NT - 1:
                        lo_next(6, BLK if p else 4 * QKV)
                    dve.wait_ge(s["ztanh"], T + 1)
                    dve.scalar_tensor_tensor(out=zg[:, :], in0=tanh_z[:, :], scalar=1.0, in1=bank(t % 2),
                                             op0=ALU.add, op1=ALU.mult).then_inc(s["zg_ok"], 1)
                    dve.wait_ge(s["y_mm"], T + 1)
                    dve.wait_ge(s["xd_ok"], T + 1)
                    if t:
                        link(dve.tensor_tensor(h8(yv[:, :]), h8(bank(6)), heads(dec[:, 1, t, :], SH, HD), ALU.mult))
                        dve.tensor_tensor(yv[:, :], yv[:, :], bank(5), ALU.add).then_inc(s["y_done"], 1)
                        dve.wait_ge(s["y_done"], T + 1)
                        link(dve.tensor_tensor(yv[:, :], yv[:, :], xd[:, :], ALU.add))
                    else:
                        dve.wait_ge(s["yT_mm"], G * NT + 1)
                        dve.tensor_tensor(yv[:, :], bank(6), xd[:, :], ALU.add).then_inc(s["y_done"], 1)
                        dve.wait_ge(s["y_done"], T + 1)
                    dve.wait_ge(s["zg_ok"], T + 1)
                    dve.tensor_tensor(yv[:, :], yv[:, :], zg[:, :], ALU.mult).then_inc(s["w_ok"], 1)
                    if t < NT - 1:
                        dve.wait_ge(s["st_mm"], G * (NT - 1) + (t + 1))
                        if t == 0:
                            dve.tensor_copy(state[:, :], bank(7)).then_inc(s["st_ok"], 1)
                        else:
                            link(dve.tensor_tensor(h8(state[:, :]), h8(state[:, :]), heads(dec[:, 2, t, :], SH, HD), ALU.mult))
                            dve.tensor_tensor(state[:, :], state[:, :], bank(7), ALU.add).then_inc(s["st_ok"], 1)
                norm_y(G * NT + (NT - 1))
                lo_next(7, BLK if p else 4 * QKV)

            with dve.Fori(0, NG // 2) as i:
                links["n"], links["base"] = 0, i * PAIR_LINKS + before
                group(i, 0)
                group(i, 1)
                assert links["n"] == PAIR_LINKS, links
            links["n"], links["base"] = before + PAIR_LINKS * (NG // 2), 0

            for k in range(KD):
                dve.wait_ge(s["split_hi"], k + 1)
                dve.tensor_tensor(rlo[:, KD + k, :], oT[:, k, :], rhi[:, KD + k, :].bitcast(F32), ALU.subtract).then_inc(s["split_lo"], 1)

            def split_y(k, count):
                dve.wait_ge(s["split_hi"], count)
                dve.scalar_tensor_tensor(out=rlo[:, k, :], in0=yT[:, k, :], scalar=par[:, 1, k:k + 1],
                                         in1=rhi[:, k, :].bitcast(F32), op0=ALU.mult, op1=ALU.subtract).then_inc(s["split_lo"], 1)

            for k in range(KD // 2):
                split_y(k, KD + k + 1)

            def gate_a(i, first=False):
                n = i * 2 + N_C1
                if not first:
                    lo(1, n + 2)
                lo(0, n + 3)
                for m in range(2):
                    dve.wait_ge(s["ga_tanh"], i * 2 + (m + 1))
                    if m == 0:
                        dve.wait_ge(s["at_mm"], i + 1)
                    else:
                        dve.wait_ge(s["blk_done"], n + 2)
                    dve.scalar_tensor_tensor(out=oT[:, bass.ds(i * 2 + m, 1), :], in0=gt[:, m:m + 1, :], scalar=1.0,
                                             in1=ps[:, 2 + m:3 + m, :], op0=ALU.add, op1=ALU.mult).then_inc(s["at_ok"], 1)

            gate_a(0, True)
            for k in range(KD // 2, KD):
                split_y(k, KD + k + 1)
            with dve.Fori(1, NG) as i:
                gate_a(i)
            for k in range(KD, KI):
                split_y(k, KD + k + 1)
            before = links["n"]
            with dve.Fori(0, NG // 2) as i:
                links["n"], links["base"] = 0, i * 4 + before
                for q in range(6):
                    r, j = divmod(q, 3)
                    n = i * 6 + (N_C2 + q)
                    lo((q + 1) % 2, n + 2)
                    if j == 2:
                        for m in range(2):
                            dve.wait_ge(s["gb_tanh"], i * 4 + (2 * r + m + 1))
                            if m == 0:
                                dve.wait_ge(s["so_mm"], i * 2 + (r + 1))
                            else:
                                dve.wait_ge(s["blk_done"], n + 1)
                            link(dve.scalar_tensor_tensor(out=tga[m], in0=tga[m], scalar=1.0, in1=bank(6 + m),
                                                          op0=ALU.add, op1=ALU.mult))
                            o_ = oT[:, bass.ds(i * 4 + (2 * r + m), 1), :]
                            dve.tensor_tensor(o_, o_, gt[:, m:m + 1, :], ALU.add).then_inc(s["so_ok"], 1)
            links["n"], links["base"] = before + 4 * (NG // 2), 0
            for k in range(KD - 2, KD):
                dve.wait_ge(s["mg_hi"], k + 1)
                dve.tensor_tensor(ulo[:, k, :], oT[:, k, :], uhi[:, k, :].bitcast(F32), ALU.subtract).then_inc(s["mg_lo2"], 1)
            for b in range(1, KD // 2):
                lo((N_D + b) % 2, N_D + b + 1)
            lo(0, N_E + 1, h=ahead_hi[0], into=ahead_lo[0])
            dve.wait_ge(s["res_in"], 48)

            def out_weighted(t):
                dve.wait_ge(s["d_sq"], t + 1)
                link(dve.tensor_tensor(two(work[:, 2 * t:2 * t + 2, :]), two(ps[:, 2 * t:2 * t + 2, :]), normw[:, 0, :], ALU.mult))

            def residual(t):
                dve.wait_ge(s["d_rstd"], t + 1)
                dve.scalar_tensor_tensor(out=resid[:, t, :], in0=two(work[:, 2 * t:2 * t + 2, :]), scalar=small[:, 28 + t:29 + t],
                                         in1=resid[:, t, :], op0=ALU.mult, op1=ALU.add).then_inc(s["d_h"], 1)

            def weigh_h(t):
                weigh(t, "hT_mm", par[:, 1, KI:KI + KD], "h_plain")

            def rest_h(t):
                rest(t, "h_hi", "h_ok")

            for t in range(2):
                out_weighted(t)
                residual(t)
            lo(1, N_E + 2, h=ahead_hi[1], into=ahead_lo[1])
            out_weighted(2)
            weigh_h(0)
            weigh_h(1)
            rest_h(0)
            rest_h(1)
            residual(2)
            out_weighted(3)
            residual(3)
            weigh_h(2)
            rest_h(2)
            weigh_h(3)
            rest_h(3)
            for q in range(2):
                lo(q, N_E + 3 + q)
            before = links["n"]
            UP_LINKS = 2 * 4

            def up(i, first=False):
                links["n"], links["base"] = 0, i * UP_LINKS + before
                for q in range(2):
                    J = i * 2 + q
                    n = J + N_E
                    for v in range(2):
                        dve.tensor_copy(fpar[:, q, :, v:v + 1], fcw[:, :, bass.ds(J + KF * v, 1)]).then_inc(s["fpar_ok"], 1)
                    for v in range(2):
                        dve.wait_ge(s["ftap"], J * 2 + (v + 1))
                        for k in range(FTAPS - 2, -1, -1):
                            sh = FTAPS - 1 - k
                            ins = dve.scalar_tensor_tensor(out=work[:, v, sh:], in0=ps[:, 2 * q + v, 0:S - sh],
                                                           scalar=fpar[:, q, k, v:v + 1], in1=work[:, v, sh:], op0=ALU.mult, op1=ALU.add)
                            if k == 0 and v == 0:
                                ins.then_inc(s["fconv"], 1)
                            else:
                                link(ins)
                    dve.wait_ge(s["ftanh"], J + 1)
                    link(dve.scalar_tensor_tensor(out=work[:, 2, :], in0=work[:, 2, :], scalar=1.0, in1=work[:, 0, :],
                                                  op0=ALU.add, op1=ALU.mult))
                    dve.wait_ge(s["flo_ok"], J)
                    dve.tensor_tensor(work[:, 3, :], work[:, 2, :], work[:, 1, :], ALU.mult).then_inc(s["f_ok"], 1)
                    dve.wait_ge(s["fhi_ok"], J + 1)
                    dve.tensor_tensor(rlo[:, bass.ds(J, 1), :], work[:, 3:4, :], rhi[:, bass.ds(J, 1), :].bitcast(F32),
                                      ALU.subtract).then_inc(s["flo_ok"], 1)
                    if not first:
                        lo(q, n + 3)
                assert links["n"] == UP_LINKS, links

            up(0, True)
            with dve.Fori(1, KF // 2) as i:
                up(i)
            links["n"], links["base"] = before + UP_LINKS * (KF // 2), 0
            for b in range(2, KF // 2):
                lo((N_F + b) % 2, N_F + b + 1)
            for t in range(NT - 1):
                wt = two(work[:, 2 * t:2 * t + 2, :])
                dve.wait_ge(s["e_sq"], t + 1)
                link(dve.tensor_tensor(wt, two(ps[:, 2 * t:2 * t + 2, :]), normw[:, 1, :], ALU.mult))
                dve.wait_ge(s["e_rstd"], t + 1)
                dve.scalar_tensor_tensor(out=wt, in0=wt, scalar=small[:, 48 + t:49 + t], in1=resid[:, t, :],
                                         op0=ALU.mult, op1=ALU.add).then_inc(s["e_ok"], 1)
            t = NT - 1
            for h in range(2):
                dve.wait_ge(s["e_sq"], NT + h)
                link(dve.tensor_tensor(work[:, 2 * t + h, :], bank(2 * t + h), normw[:, 1, 512 * h:512 * h + 512], ALU.mult))
            dve.wait_ge(s["e_rstd"], NT)
            for h in range(2):
                dve.scalar_tensor_tensor(out=work[:, 2 * t + h, :], in0=work[:, 2 * t + h, :], scalar=small[:, 48 + t:49 + t],
                                         in1=resid[:, t, 512 * h:512 * h + 512], op0=ALU.mult, op1=ALU.add).then_inc(s["e_ok"], 1)

        @block.tensor
        def _(pe):
            def tiles(w, k):
                return w.rearrange("p (k n) -> p k n", k=k)

            def features(b, sl, m, acts, first=True, last=True, span=slice(0, S), split=None):
                hi_, lo_ = (tiles(w, KD) for w in split or (whi[sl][:, :], wlo[sl][:, :]))
                for k in range(KD):
                    ah, al = acts(k)
                    c = slice(m * P, (m + 1) * P)
                    pe.matmul(bank(b)[:, span], hi_[:, k, c], ah[:, span], start=first and k == 0, stop=False)
                    pe.matmul(bank(b)[:, span], hi_[:, k, c], al[:, span], start=False, stop=False)
                    ins = pe.matmul(bank(b)[:, span], lo_[:, k, c], ah[:, span], start=False, stop=last and k == KD - 1)
                return ins

            def tokens(o, ah, al, wh, wl, first, last):
                pe.matmul(o, ah, wh, start=first, stop=False)
                pe.matmul(o, al, wh, start=False, stop=False)
                return pe.matmul(o, ah, wl, start=False, stop=last)

            def u(k):
                return uhi[:, k, :], ulo[:, k, :]

            def turn_tile(t, src, done):
                for k in range(KD):
                    ins = pe.transpose(ps[:, 2 * t + k // 4, (k % 4) * P:(k % 4 + 1) * P], src[:, k * P:(k + 1) * P], ident[:, :])
                ins.then_inc(s[done], 1)

            pe.wait_ge(s["pool_c"], HALF + 1)
            pe.wait_ge(s["par_in"], 16 * 2)
            pe.transpose(ps[:, 7, 0:KD], nrow[:, :], ident[0:KD, 0:KD]).then_inc(s["parT_mm"], 1)
            pe.wait_ge(s["dve_chain"], 3)
            pe.transpose(ps[:, 7, KD:KD + NT], rtmp[0:NT, 0:P], ident[0:NT, 0:NT]).then_inc(s["parT_mm"], 1)
            for t in range(NT):
                pe.wait_ge(s["xn"], t + 1)
                if t == NT - 1:
                    pe.wait_ge(s["par_ok"], 1)
                    pe.wait_ge(s["posT_ok"], 1)
                turn_tile(t, xin[:, t, :], "xT_mm")
            pe.wait_ge(s["par2_in"], 16 * 10)
            pe.wait_ge(s["u_plain"], 2)
            pe.transpose(ps[:, 3, 0:NR1], prow[0:NR1, 1, :], ident[0:NR1, 0:NR1]).then_inc(s["parT_mm"], 1)
            pe.transpose(ps[:, 3, NR1:NR1 + P], prow[:, 2, :], ident[:, :]).then_inc(s["parT_mm"], 1)
            pe.transpose(ps[:, 3, NR1 + P:NR1 + P + NCP], prow[0:NCP, 0, :], ident[0:NCP, 0:NCP]).then_inc(s["parT_mm"], 1)

            def turn_y(b):
                for f in range(4):
                    ins = pe.transpose(ps[:, b, f * P:(f + 1) * P], yv[:, f * P:(f + 1) * P], ident[:, :])
                ins.then_inc(s["yT_mm"], 1)

            def group(i, p):
                G = i * 2 + p
                Q0 = PER_G * p

                def block_ready(j):
                    pe.wait_ge(s["lo_done"], G * PER_G + (j + 1))
                    return (Q0 + j) % 2

                pe.wait_ge(s["yT_sb"], G * NT)
                for h in range(2):
                    sl = block_ready(h)
                    wh, wl = (w[sl][:, 0:4 * QKV].rearrange("p (k n) -> p k n", k=4) for w in (whi, wlo))
                    for t in range(NT):
                        c = slice(t * P, (t + 1) * P)
                        pe.wait_ge(s["u_ok"] if h == 0 else s["u2_ok"], t + 1)
                        if h == 0 and t == 1:
                            pe.wait_ge(s["zg_ok"], G * NT)
                        if h == 0 and t == NT - 1:
                            pe.wait_ge(s["par_ok"], 5)
                        for k in range(4):
                            ins = tokens(bank(t, QKV), uhi[:, 4 * h + k, c], ulo[:, 4 * h + k, c], wh[:, k, :], wl[:, k, :],
                                         h == 0 and k == 0, h == 1 and k == 3)
                        if t == NT - 1:
                            ins.then_inc(s["blk_done"], 1)
                        elif h == 1:
                            ins.then_inc(s["qkv_mm"], 1)
                    if h == 0:
                        pe.wait_ge(s["yn_ok"], G * NT)
                        pe.wait_ge(s["st_ok"], G * (NT - 1))
                        turn_y(7)

                def conv_tiles(j):
                    sl = block_ready(j)
                    for m in range(2):
                        f = 2 * (j - 2) + m
                        if f == 0:
                            pe.wait_ge(s["o_sb"], G * NT)
                        elif f == 1:
                            pe.wait_ge(s["y_done"], G * NT)
                        elif f == 3:
                            pe.wait_ge(s["yT_sb"], G * NT + 1)
                        elif f >= 4:
                            pe.wait_ge(s["conv_ok"], G * 6 + (f - 3))
                        features(4 + f % 4, sl, m, u).then_inc(s["conv_mm"] if m == 0 else s["blk_done"], 1)

                conv_tiles(2)
                conv_tiles(3)
                conv_tiles(4)
                pe.wait_ge(s["qkv_sb"], G * NT + NT)
                pe.wait_ge(s["roped"], G * NT + NT)
                for j in range(3):
                    for t in range(NT):
                        ins = pe.transpose(ps[:, j, t * P:(t + 1) * P], qk_rot[:, t, j * P:(j + 1) * P], ident[:, :])
                    ins.then_inc(s["qkT_mm"], 1)
                pe.wait_ge(s["dt_ok"], G + 1)
                for j, m in enumerate((above_f, tri, ones)):
                    ins = pe.matmul(ps[:, 3, j * NT * SH:(j + 1) * NT * SH], m[:, :], adt[:, :], start=True, stop=True)
                ins.then_inc(s["decay_mm"], 1)

                def tok(f):
                    pe.wait_ge(s["silu_ok"], G * 6 + (1 if f == 0 else f + 2))
                    if f < 2:
                        pe.wait_ge(s["qkT_sb"], G * 3 + (f + 1))
                    elif f == 2:
                        pe.wait_ge(s["tok_sb"], G * 5 + 2)
                    elif f == 3:
                        pe.wait_ge(s["conv_ok"], G * 6 + 4)
                    else:
                        pe.wait_ge(s["cbm_ok"], G * NT + 1)
                    for t in range(NT):
                        ins = pe.transpose(ps[:, TOK_BANK[f], t * P:(t + 1) * P], conv[:, f + (f > 0), t * P:(t + 1) * P], ident[:, :])
                    ins.then_inc(s["tok_mm"], 1)

                tok(0)
                tok(1)

                for t in range(NT):
                    T = G * NT + t
                    c = slice(t * P, (t + 1) * P)

                    def sums(t):
                        T = G * NT + t
                        if t == 0:
                            pe.wait_ge(s["qkT_sb"], G * 3 + 3)
                            pe.wait_ge(s["decay_ok"], G + 1)
                        else:
                            pe.wait_ge(s["lexp"], T * 2)
                            pe.wait_ge(s["yT_sb"], G * NT + t)
                        for q in range(2):
                            pe.wait_ge(s["seg_hi_ok"], T * SH + 4 * (q + 1))
                            pe.wait_ge(s["seg_lo_ok"], T * 2 + (q + 1))
                            pe.matmul(bank(2 + q), above[:, :], seg_hi[:, q, :], start=True, stop=False)
                            pe.matmul(bank(2 + q), above[:, :], seg_lo[:, q, :], start=False, stop=True).then_inc(s["seg_mm"], 1)

                    if t != 1:
                        sums(t)
                    pe.wait_ge(s["silu_ok"], G * 6 + 2)
                    if t == 0:
                        pe.wait_ge(s["conv_ok"], G * 6 + 3)
                    else:
                        pe.wait_ge(s["y_done"], T)
                    pe.matmul(bank(6, P), conv[:, 0, c], conv[:, 1, c], start=True, stop=True).then_inc(s["cb_mm"], 1)
                    def scores():
                        pe.wait_ge(s["qkT_sb"], G * 3 + 3)
                        if t:
                            pe.wait_ge(s["o_sb"], T)
                        else:
                            pe.wait_ge(s["conv_ok"], G * 6 + 6)
                        for h in range(QH):
                            r = slice((h % 2) * 64, (h % 2) * 64 + 64)
                            b, o = 4 + h % 2, (h // 2) * P
                            ins = pe.matmul(ps[:, b, o:o + P], qT[r, h // 2, c], kT[r, c], start=True, stop=True)
                            if t:
                                ins = pe.matmul(ps[0:64, b, o + 64:o + P], qT[r, h // 2, t * P:t * P + 64],
                                                kT[r, t * P - 64:t * P], start=True, stop=True)
                        ins.then_inc(s["s_mm"], 1)

                    def turn_p():
                        pe.wait_ge(s["p_ok"], T + 1)
                        for h in range(QH):
                            ins = pe.transpose(ps[:, 4, h * P:(h + 1) * P], probs[:, h, 0:P], ident[:, :])
                        ins.then_inc(s["pT_mm"], 1)

                    def z_tile(halves=range(2)):
                        zb = t % 2
                        if t == 0:
                            pe.wait_ge(s["tok_sb"], G * 5 + 1)
                        elif t == 1:
                            pe.wait_ge(s["tok_sb"], G * 5 + 5)
                        else:
                            pe.wait_ge(s["zg_ok"], T - 1)
                        for h in halves:
                            sl = block_ready(5 + h)
                            wh, wl = tiles(whi[sl][:, :], 4), tiles(wlo[sl][:, :], 4)
                            for k in range(4):
                                ins = tokens(bank(zb), uhi[:, 4 * h + k, c], ulo[:, 4 * h + k, c], wh[:, k, :], wl[:, k, :],
                                             h == 0 and k == 0, h == 1 and k == 3)
                            if t == NT - 1:
                                ins.then_inc(s["blk_done"], 1)
                            elif h:
                                ins.then_inc(s["z_mm"], 1)

                    if t == 0:
                        z_tile((0,))
                        scores()
                        for f in range(2, 5):
                            tok(f)
                        z_tile((1,))
                    else:
                        scores()
                        z_tile()
                        pe.wait_ge(s["lexp"], T * 2 + 2)
                        pe.wait_ge(s["yn_ok"], T)
                        turn_y(3)
                        turn_p()
                    pe.wait_ge(s["m_ok"], T * 2 + 2)
                    pe.wait_ge(s["xdt_ok"], T + 1)
                    if t:
                        pe.wait_ge(s["st_ok"], G * (NT - 1) + t)
                        pe.matmul(bank(6), conv[:, 1, c], state[:, :], start=True, stop=True)
                        pe.wait_ge(s["smx"], T + 1)
                    for h in range(SH):
                        c_ = slice(h * HD, (h + 1) * HD)
                        ins = pe.matmul(ps[:, 5 if t else 6, c_], decay_m[:, h, :], xdt[:, c_], start=True, stop=True)
                    ins.then_inc(s["y_mm"], 1)
                    if t == 0:
                        sums(1)
                        turn_p()
                    if t < NT - 1:
                        pe.wait_ge(s["xdtd_ok"], T + 1)
                        if t:
                            pe.wait_ge(s["st_ok"], G * (NT - 1) + t)
                        else:
                            pe.wait_ge(s["tok_sb"], G * 5 + 5)
                        pe.matmul(bank(7), b_tok[:, c], xdtd[:, :], start=True, stop=True).then_inc(s["st_mm"], 1)
                    pe.wait_ge(s["pT_sb"], T + 1)
                    pe.wait_ge(s["va_ok"], T * 2 + 2)
                    for h in range(QH):
                        r = slice((h % 2) * 64, (h % 2) * 64 + 64)
                        for half in (1, 0):
                            o = ps[r, 4, (h // 2) * P + 64 * half:(h // 2) * P + 64 * half + 64]
                            n = 64 if t == 0 and half == 0 else P
                            v = qkv_sb[0:n, t, QW + KW:QW + 2 * KW] if half else va[0:n, t, :]
                            ins = pe.matmul(o, v, pT[0:n, (h % 2) * 2 + h // 2, 64 * half:64 * half + 64], start=True, stop=True)
                    ins.then_inc(s["o_mm"], 1)

            with pe.Fori(0, NG // 2) as i:
                group(i, 0)
                group(i, 1)

            pe.wait_ge(s["zg_ok"], NG * NT)
            pe.wait_ge(s["lexp"], 2 * NG * NT)
            pe.wait_ge(s["yT_sb"], NG * NT)

            def gate_a(i, first=False):
                n = i * 2 + N_C1
                pe.wait_ge(s["lo_done"], n + 1)
                pe.wait_ge(s["ga_tanh"], i * 2)
                features(0, 0, 0, u).then_inc(s["ga_mm"], 1)
                features(1, 0, 1, u).then_inc(s["blk_done"], 1)
                if first:
                    pe.wait_ge(s["yn_ok"], NG * NT)
                    pe.wait_ge(s["st_ok"], NG * (NT - 1))
                    turn_y(7)
                pe.wait_ge(s["lo_done"], n + 2)
                pe.wait_ge(s["at_ok"], i * 2)

                def o(k):
                    if first:
                        pe.wait_ge(s["split_lo"], k + 1)
                    return rhi[:, KD + k, :], rlo[:, KD + k, :]

                features(2, 1, 0, o).then_inc(s["at_mm"], 1)
                features(3, 1, 1, o).then_inc(s["blk_done"], 1)

            gate_a(0, True)
            with pe.Fori(1, NG) as i:
                gate_a(i)
            pe.wait_ge(s["o_sb"], NG * NT)
            pe.wait_ge(s["y_done"], NG * NT)
            pe.wait_ge(s["yT_sb"], NG * NT + 1)
            with pe.Fori(0, NG // 2) as i:
                for q in range(6):
                    r, j = divmod(q, 3)
                    pe.wait_ge(s["lo_done"], i * 6 + (N_C2 + q + 1))
                    if j == 0:
                        pe.wait_ge(s["gb_tanh"], i * 4 + 2 * r)
                        features(4, q % 2, 0, u).then_inc(s["gb_mm"], 1)
                        features(5, q % 2, 1, u).then_inc(s["blk_done"], 1)
                    elif j == 1:
                        pe.wait_ge(s["so_ok"], i * 4 + 2 * r)
                        y = lambda k: (rhi[:, k, :], rlo[:, k, :])
                        features(6, q % 2, 0, y, True, False)
                        features(7, q % 2, 1, y, True, False).then_inc(s["blk_done"], 1)
                    else:
                        pe.wait_ge(s["split_lo"], KD + KI)
                        y = lambda k: (rhi[:, KD + k, :], rlo[:, KD + k, :])
                        features(6, q % 2, 0, y, False, True).then_inc(s["so_mm"], 1)
                        features(7, q % 2, 1, y, False, True).then_inc(s["blk_done"], 1)

            def all_tokens(n, n0, acts_hi, acts_lo, tile_ok, bank_ok, done, between=lambda t, b: None):
                def part(b, k, t, halves=range(2)):
                    wh, wl = tiles(whi[b % 2][:, :], 2), tiles(wlo[b % 2][:, :], 2)
                    c = slice(t * P, (t + 1) * P)
                    for h in halves:
                        if b == 0 and k == 0:
                            bank_ok(2 * t + h)
                        ins = tokens(bank(2 * t + h), acts_hi[:, 2 * b + k, c], acts_lo[:, 2 * b + k, c],
                                     wh[:, k, 512 * h:512 * h + 512], wl[:, k, 512 * h:512 * h + 512],
                                     b == 0 and k == 0, b == n - 1 and k == 1)
                    return ins

                def ready(b):
                    pe.wait_ge(s["lo_done"], n0 + b + 1)
                    tile_ok(2 * b + 2)

                for b in range(n - 2):
                    ready(b)
                    for t in order:
                        for k in range(2):
                            ins = part(b, k, t)
                    ins.then_inc(s["blk_done"], 1)
                for t, b in ((0, n - 2), (1, n - 2), (0, n - 1), (1, n - 1), (2, n - 2), (2, n - 1)):
                    if t == 0:
                        ready(b)
                    for k in range(2):
                        ins = part(b, k, t)
                    if b == n - 1:
                        ins.then_inc(s[done], 1)
                    between(t, b)
                for h in range(2):
                    for b in (n - 2, n - 1):
                        for k in range(2):
                            ins = part(b, k, NT - 1, (h,))
                        if h == 1:
                            ins.then_inc(s["blk_done"], 1)
                    if h == 0:
                        ins.then_inc(s[done], 1)
                        between(NT - 1, n - 1)

            def bank_ok(b):
                if b >= 6:
                    pe.wait_ge(s["so_ok"], KD)

            order = range(NT)

            def turn_h(t):
                pe.wait_ge(s["hn_ok"], t + 1)
                turn_tile(t, two(work[:, 2 * t:2 * t + 2, :]), "hT_mm")

            def between(t, b):
                if (t, b) == (NT - 2, KD // 2 - 1):
                    turn_h(0)
                if (t, b) == (NT - 1, KD // 2 - 1):
                    turn_h(1)

            def merged_ok(k):
                pe.wait_ge(s["mg_lo"] if k <= KD - 2 else s["mg_lo2"], k if k <= KD - 2 else k - (KD - 2))

            all_tokens(KD // 2, N_D, uhi, ulo, merged_ok, bank_ok, "out_mm", between)

            half = slice(0, S // 2), slice(S // 2, S)
            for q in range(2):
                pe.wait_ge(s["lo_done"], N_E + q + 1)
                pe.wait_ge(s["h_ok"], NT // 2)
                for m in range(2):
                    features(2 * q + m, q, m, u, span=half[0], split=(ahead_hi[q], ahead_lo[q]))
                    if q != m:
                        turn_h(NT // 2 + q)
            for q in range(2):
                pe.wait_ge(s["h_ok"], NT)
                features(2 * q, q, 0, u, span=half[1], split=(ahead_hi[q], ahead_lo[q])).then_inc(s["up_mm"], 1)
                features(2 * q + 1, q, 1, u, span=half[1], split=(ahead_hi[q], ahead_lo[q])).then_inc(s["blk_done"], 1)

            def up(i):
                for q in range(2):
                    J = i * 2 + q
                    pe.wait_ge(s["lo_done"], J + (N_E + 1))
                    pe.wait_ge(s["f_ok"], J - 1)
                    features(2 * q, q, 0, u).then_inc(s["up_mm"], 1)
                    features(2 * q + 1, q, 1, u).then_inc(s["blk_done"], 1)

            with pe.Fori(1, KF // 2) as i:
                up(i)
            order = (3, 2, 0, 1)

            def bank_ok(b):
                if b < 4:
                    pe.wait_ge(s["f_ok"], KF - 1 + b // 2)

            all_tokens(KF // 2, N_F, rhi, rlo, lambda k: pe.wait_ge(s["flo_ok"], k), bank_ok, "dn_mm")


def bass_f32_inverse(k, width):
    import numpy as np
    return np.float32(1.0) / np.float32(ROPE_THETA ** (2.0 * k / width))


PAIR_LINKS = 150

_INS = ['x', 'positions', 'mix_pre_norm', 'w_in', 'attn_sinks', 'ssd_conv_w', 'ssd_conv_b', 'ssd_dt_bias',
        'ssd_a_log', 'ssd_d', 'ssd_norm', 'w_attn_out', 'w_ssd_out', 'w_out', 'mix_post_norm',
        'ffn_pre_norm', 'w_up', 'ffn_conv_w', 'ffn_conv_b', 'w_down', 'ffn_post_norm']


def kernel(**inputs):
    import numpy as _np
    import concourse.bacc as _bacc
    from concourse import mybir as _mybir
    from concourse.bass_utils import run_bass_kernel_spmd as _run

    nc = _bacc.Bacc("TRN2", target_bir_lowering=False, num_devices=1, dynamic_dma_scratch_size=1024)
    arrays, args = {}, []
    for name in _INS:
        a = _np.ascontiguousarray(inputs[name])
        arrays[f"in_{name}_dram"] = a
        args.append(nc.dram_tensor(f"in_{name}_dram", a.shape, _mybir.dt.from_np(a.dtype), kind="ExternalInput").ap())
    shape = tuple(inputs["x"].shape)
    args.append(nc.dram_tensor("out_0_dram", shape, _mybir.dt.float32, kind="ExternalOutput").ap())
    hybrid_block(nc, *args)
    r = _run(nc, [arrays], core_ids=[0])
    return r.results[0]["out_0_dram"]
```
